# Optimizing a Trainium2 kernel written in Bass

```python
import numpy as np
import jax, jax.numpy as jnp
from jax import lax
import math

D_MODEL = 1024
BATCH = 1
SEQ = 512
DEPTH = 2

HEAD_DIM = 64
N_A_LAYERS = DEPTH // 2
N_B_LAYERS = DEPTH - N_A_LAYERS
MEM_LEN = 256
MEM_HEADS = 4
MEM_W = MEM_HEADS * HEAD_DIM
CONV_W = D_MODEL - MEM_W
CONV_K = 31
NSA_HEADS = (D_MODEL - MEM_W) // HEAD_DIM
NSA_W = NSA_HEADS * HEAD_DIM
NSA_KV_GROUPS = 2
HEADS_PER_GROUP = NSA_HEADS // NSA_KV_GROUPS
CMP_L = 32
CMP_STRIDE = 16
CMP_HID = 256
SEL_L = 64
N_SEL = 16
WIN = 512
Q_BLOCK = 128
D_FF = 4 * D_MODEL
KV_W = 6 * NSA_KV_GROUPS * HEAD_DIM
A_IN_W = 2 * CONV_W + MEM_W
B_IN_W = NSA_W + MEM_W + 3 * NSA_HEADS


def rms_norm(x, g, eps=1e-6):
    xf = x.astype(jnp.float32)
    y = xf * lax.rsqrt(jnp.mean(xf * xf, axis=-1, keepdims=True) + eps)
    return (y * g.astype(jnp.float32)).astype(x.dtype)

def layer_norm(x, g, b, eps=1e-5):
    xf = x.astype(jnp.float32)
    mu = jnp.mean(xf, axis=-1, keepdims=True)
    var = jnp.mean(jnp.square(xf - mu), axis=-1, keepdims=True)
    y = (xf - mu) * lax.rsqrt(var + eps)
    return (y * g.astype(jnp.float32) + b.astype(jnp.float32)).astype(x.dtype)

def masked_softmax(s, mask):
    s = jnp.where(mask, s.astype(jnp.float32), -jnp.inf)
    m = jnp.max(s, axis=-1, keepdims=True)
    m = jnp.where(jnp.isfinite(m), m, 0.0)
    e = jnp.exp(s - m)
    return e / jnp.maximum(jnp.sum(e, axis=-1, keepdims=True), 1e-30)

def selection_map(n_cmp, n_sb):
    cs = np.arange(n_cmp)[:, None] * CMP_STRIDE
    ss = np.arange(n_sb)[None, :] * SEL_L
    ov = np.minimum(cs + CMP_L, ss + SEL_L) - np.maximum(cs, ss)
    return (np.clip(ov, 0, None) / CMP_STRIDE).astype(np.float32)

def squared_relu_mlp(h, w_in, w_out):
    return jnp.square(jax.nn.relu(h @ w_in)) @ w_out

def memory_attention(q, mk, mv):
    B, S = q.shape[:2]
    s = jnp.einsum('bshd,bmhd->bhsm', q, mk) * HEAD_DIM ** -0.5
    p = jax.nn.softmax(s.astype(jnp.float32), axis=-1)
    return jnp.einsum('bhsm,bmhd->bshd', p.astype(mv.dtype), mv).reshape(B, S, MEM_W)

def conformer_conv(u, dw, dw_b, ln_g, ln_b):
    a, gate = jnp.split(u, 2, axis=-1)
    v = a * jax.nn.sigmoid(gate)
    v = lax.conv_general_dilated(v, dw[:, None, :], window_strides=(1,),
                                 padding=[(CONV_K - 1, 0)],
                                 dimension_numbers=('NWC', 'WIO', 'NWC'),
                                 feature_group_count=CONV_W) + dw_b
    return jax.nn.silu(layer_norm(v, ln_g, ln_b))

def shared_nsa_kv(h, kv_norm_g, w_kv, k_norm_g, pe_k, pe_v, w1_k, w2_k, w1_v, w2_v):
    B, S = h.shape[:2]
    G, HD = NSA_KV_GROUPS, HEAD_DIM
    kv = (rms_norm(h, kv_norm_g) @ w_kv).reshape(B, S, 6, G, HD)
    k_c, v_c, k_s, v_s, k_w, v_w = (kv[:, :, i] for i in range(6))
    n_cmp = (S - CMP_L) // CMP_STRIDE + 1
    idx = np.arange(n_cmp)[:, None] * CMP_STRIDE + np.arange(CMP_L)[None, :]

    def compress(t, pe, w1, w2):
        blk = t[:, idx] + pe[:, None, :]
        blk = blk.transpose(0, 1, 3, 2, 4).reshape(B, n_cmp, G, CMP_L * HD)
        return jax.nn.gelu(blk @ w1) @ w2

    k_cmp = rms_norm(compress(k_c, pe_k, w1_k, w2_k), k_norm_g[0])
    v_cmp = compress(v_c, pe_v, w1_v, w2_v)
    n_sb = S // SEL_L
    k_blk = rms_norm(k_s, k_norm_g[1]).reshape(B, n_sb, SEL_L, G, HD).transpose(0, 3, 1, 2, 4)
    v_blk = v_s.reshape(B, n_sb, SEL_L, G, HD).transpose(0, 3, 1, 2, 4)
    pad = ((0, 0), (WIN, 0), (0, 0), (0, 0))
    k_win = jnp.pad(rms_norm(k_w, k_norm_g[2]), pad)
    v_win = jnp.pad(v_w, pad)
    return k_cmp, v_cmp, k_blk, v_blk, k_win, v_win

def nsa_attention(q, gates, k_cmp, v_cmp, k_blk, v_blk, k_win, v_win):
    B, S = q.shape[:2]
    G, HG, HD = NSA_KV_GROUPS, HEADS_PER_GROUP, HEAD_DIM
    n_qb = S // Q_BLOCK
    n_cmp = k_cmp.shape[1]
    n_sb = k_blk.shape[2]
    n_sel = min(N_SEL, n_sb)
    scale = HD ** -0.5
    cmp_end = jnp.asarray(np.arange(n_cmp) * CMP_STRIDE + CMP_L - 1)
    sel_map = jnp.asarray(selection_map(n_cmp, n_sb))
    blk_ids = jnp.arange(n_sb)
    b_ix = jnp.arange(B)[:, None, None, None]
    g_ix = jnp.arange(G)[None, None, :, None]
    qs = q.reshape(B, n_qb, Q_BLOCK, G, HG, HD).transpose(1, 0, 2, 3, 4, 5)
    gs = gates.reshape(B, n_qb, Q_BLOCK, G, HG, 3).transpose(1, 0, 2, 3, 4, 5)

    def block(args):
        c, qb, gb = args
        t = c * Q_BLOCK + jnp.arange(Q_BLOCK)
        s = jnp.einsum('bqghd,bngd->bqghn', qb, k_cmp) * scale
        p_cmp = masked_softmax(s, (cmp_end[None, :] <= t[:, None])[None, :, None, None, :])
        o_cmp = jnp.einsum('bqghn,bngd->bqghd', p_cmp.astype(v_cmp.dtype), v_cmp)
        imp = jnp.einsum('bqgn,nj->bqgj', jnp.sum(p_cmp, axis=3), sel_map)
        tb = (t // SEL_L)[:, None]
        valid = (blk_ids[None, :] <= tb)[None, :, None, :]
        forced = ((blk_ids[None, :] == 0) | (blk_ids[None, :] == tb)
                  | (blk_ids[None, :] == tb - 1))[None, :, None, :]
        score = jnp.where(forced, jnp.inf, jnp.where(valid, imp, -jnp.inf))
        top_val, top_idx = lax.top_k(score, n_sel)
        kg = k_blk[b_ix, g_ix, top_idx]
        vg = v_blk[b_ix, g_ix, top_idx]
        pos = top_idx[..., None] * SEL_L + jnp.arange(SEL_L)
        smask = (top_val > -jnp.inf)[..., None] & (pos <= t[None, :, None, None, None])
        s = jnp.einsum('bqghd,bqgnkd->bqghnk', qb, kg) * scale
        n_tok = n_sel * SEL_L
        p = masked_softmax(s.reshape(B, Q_BLOCK, G, HG, n_tok),
                           smask.reshape(B, Q_BLOCK, G, 1, n_tok))
        o_slc = jnp.einsum('bqghm,bqgmd->bqghd', p.astype(vg.dtype),
                           vg.reshape(B, Q_BLOCK, G, n_tok, HD))
        kw = lax.dynamic_slice_in_dim(k_win, c * Q_BLOCK, Q_BLOCK + WIN, axis=1)
        vw = lax.dynamic_slice_in_dim(v_win, c * Q_BLOCK, Q_BLOCK + WIN, axis=1)
        kp = c * Q_BLOCK - WIN + jnp.arange(Q_BLOCK + WIN)
        wmask = (kp[None, :] <= t[:, None]) & (kp[None, :] > t[:, None] - WIN) & (kp[None, :] >= 0)
        s = jnp.einsum('bqghd,bkgd->bqghk', qb, kw) * scale
        p = masked_softmax(s, wmask[None, :, None, None, :])
        o_win = jnp.einsum('bqghk,bkgd->bqghd', p.astype(vw.dtype), vw)
        o = o_cmp * gb[..., 0:1] + o_slc * gb[..., 1:2] + o_win * gb[..., 2:3]
        return o.reshape(B, Q_BLOCK, NSA_W)

    out = lax.map(block, (jnp.arange(n_qb), qs, gs))
    return out.transpose(1, 0, 2, 3).reshape(B, S, NSA_W)

def first_inputs(seed: int = 0) -> dict:
    key = jax.random.key(seed)
    ks = iter(jax.random.split(key, 32))

    def w(shape, fan_in):
        return jax.random.normal(next(ks), shape, jnp.float32) * fan_in ** -0.5

    def gain(shape):
        return 1.0 + 0.1 * jax.random.normal(next(ks), shape, jnp.float32)

    def bias(shape):
        return 0.01 * jax.random.normal(next(ks), shape, jnp.float32)

    return {
        'x': jax.random.normal(next(ks), (BATCH, SEQ, D_MODEL), jnp.float32),
        'mem': jax.random.normal(next(ks), (BATCH, MEM_LEN, D_MODEL), jnp.float32),
        'norm_mix_g': gain((DEPTH, D_MODEL)),
        'norm_mlp_g': gain((DEPTH, D_MODEL)),
        'mem_norm_g': gain((D_MODEL,)),
        'w_mem_kv': w((DEPTH, D_MODEL, 2 * MEM_W), D_MODEL),
        'mem_q_norm_g': gain((DEPTH, HEAD_DIM)),
        'mem_k_norm_g': gain((DEPTH, HEAD_DIM)),
        'w_out': w((DEPTH, D_MODEL, D_MODEL), D_MODEL),
        'w_mlp_in': w((DEPTH, D_MODEL, D_FF), D_MODEL),
        'w_mlp_out': w((DEPTH, D_FF, D_MODEL), D_FF),
        'a_w_in': w((N_A_LAYERS, D_MODEL, A_IN_W), D_MODEL),
        'a_b_glu': bias((N_A_LAYERS, 2 * CONV_W)),
        'a_dw': w((N_A_LAYERS, CONV_K, CONV_W), CONV_K),
        'a_dw_b': bias((N_A_LAYERS, CONV_W)),
        'a_ln_g': gain((N_A_LAYERS, CONV_W)),
        'a_ln_b': bias((N_A_LAYERS, CONV_W)),
        'b_w_in': w((N_B_LAYERS, D_MODEL, B_IN_W), D_MODEL),
        'b_gate_b': bias((N_B_LAYERS, 3 * NSA_HEADS)),
        'b_q_norm_g': gain((N_B_LAYERS, HEAD_DIM)),
        'kv_norm_g': gain((D_MODEL,)),
        'w_kv': w((D_MODEL, KV_W), D_MODEL),
        'k_norm_g': gain((3, HEAD_DIM)),
        'cmp_pe_k': 0.1 * jax.random.normal(next(ks), (CMP_L, HEAD_DIM), jnp.float32),
        'cmp_pe_v': 0.1 * jax.random.normal(next(ks), (CMP_L, HEAD_DIM), jnp.float32),
        'cmp_w1_k': w((CMP_L * HEAD_DIM, CMP_HID), CMP_L * HEAD_DIM),
        'cmp_w2_k': w((CMP_HID, HEAD_DIM), CMP_HID),
        'cmp_w1_v': w((CMP_L * HEAD_DIM, CMP_HID), CMP_L * HEAD_DIM),
        'cmp_w2_v': w((CMP_HID, HEAD_DIM), CMP_HID),
    }

def first_block(x, mem, norm_mix_g, norm_mlp_g, mem_norm_g, w_mem_kv, mem_q_norm_g, mem_k_norm_g,
              w_out, w_mlp_in, w_mlp_out, a_w_in, a_b_glu, a_dw, a_dw_b, a_ln_g, a_ln_b,
              b_w_in, b_gate_b, b_q_norm_g, kv_norm_g, w_kv, k_norm_g, cmp_pe_k, cmp_pe_v,
              cmp_w1_k, cmp_w2_k, cmp_w1_v, cmp_w2_v):
    B, S = x.shape[:2]
    mem_n = rms_norm(mem, mem_norm_g)
    shared = None
    for l in range(DEPTH):
        mkv = (mem_n @ w_mem_kv[l]).reshape(B, MEM_LEN, 2, MEM_HEADS, HEAD_DIM)
        mk = rms_norm(mkv[:, :, 0], mem_k_norm_g[l])
        mv = mkv[:, :, 1]
        h = rms_norm(x, norm_mix_g[l])
        if l == N_A_LAYERS:
            shared = shared_nsa_kv(x, kv_norm_g, w_kv, k_norm_g, cmp_pe_k, cmp_pe_v,
                                   cmp_w1_k, cmp_w2_k, cmp_w1_v, cmp_w2_v)
        if l < N_A_LAYERS:
            i = l
            u = h @ a_w_in[i]
            conv_out = conformer_conv(u[..., :2 * CONV_W] + a_b_glu[i], a_dw[i], a_dw_b[i],
                                      a_ln_g[i], a_ln_b[i])
            qm = rms_norm(u[..., 2 * CONV_W:].reshape(B, S, MEM_HEADS, HEAD_DIM), mem_q_norm_g[l])
            mix = jnp.concatenate([conv_out, memory_attention(qm, mk, mv)], axis=-1)
        else:
            i = l - N_A_LAYERS
            u = h @ b_w_in[i]
            q = rms_norm(u[..., :NSA_W].reshape(B, S, NSA_HEADS, HEAD_DIM), b_q_norm_g[i])
            qm = rms_norm(u[..., NSA_W:NSA_W + MEM_W].reshape(B, S, MEM_HEADS, HEAD_DIM),
                          mem_q_norm_g[l])
            gates = jax.nn.sigmoid(u[..., NSA_W + MEM_W:] + b_gate_b[i]).reshape(B, S, NSA_HEADS, 3)
            nsa_out = nsa_attention(q, gates, *shared)
            mix = jnp.concatenate([nsa_out, memory_attention(qm, mk, mv)], axis=-1)
        x = x + mix @ w_out[l]
        x = x + squared_relu_mlp(rms_norm(x, norm_mlp_g[l]), w_mlp_in[l], w_mlp_out[l])
    return x


DEPTH_2 = 1

RWKV_HEADS = 8
RWKV_WIDTH = RWKV_HEADS * HEAD_DIM
ATT_Q_HEADS = 8
ATT_KV_HEADS = 2
ATT_GROUP = ATT_Q_HEADS // ATT_KV_HEADS
ATT_WIDTH = ATT_Q_HEADS * HEAD_DIM
KV_WIDTH = ATT_KV_HEADS * HEAD_DIM
WINDOW = 128
BLOCK = 128
DECAY_LORA = 32
ICLR_LORA = 32
GATE_LORA = 96
D_FF_2 = 2816
N_BRANCH = 2
RMS_EPS = 1e-6
GN_EPS = 64e-5

RWKV_COLS = 3 * RWKV_WIDTH + DECAY_LORA + ICLR_LORA + GATE_LORA
ATT_COLS = ATT_WIDTH + 2 * KV_WIDTH
GATE_COLS = N_BRANCH * D_MODEL
IN_COLS = RWKV_COLS + ATT_COLS + GATE_COLS


def rms_norm_2(x, g, eps=RMS_EPS):
    xf = x.astype(jnp.float32)
    y = xf * lax.rsqrt(jnp.mean(xf * xf, axis=-1, keepdims=True) + eps)
    return (y * g.astype(jnp.float32)).astype(x.dtype)

def swiglu(h, w_gate, w_up, w_down):
    return (jax.nn.silu(h @ w_gate) * (h @ w_up)) @ w_down

def token_shift(p):
    return jnp.pad(p, ((0, 0), (1, 0), (0, 0)))[:, :-1]

def wkv7_scan(r, w, k, v, a, b):
    Bsz, T, H, N = r.shape
    xs = tuple(jnp.moveaxis(t, 1, 0) for t in (r, w, k, v, a, b))

    def step(S, inp):
        r_t, w_t, k_t, v_t, a_t, b_t = inp
        sa = jnp.einsum('bhij,bhj->bhi', S, a_t)
        S = S * w_t[:, :, None, :] + sa[..., None] * b_t[:, :, None, :] + v_t[..., None] * k_t[:, :, None, :]
        y_t = jnp.einsum('bhij,bhj->bhi', S, r_t)
        return S, y_t

    S0 = jnp.zeros((Bsz, H, N, N), jnp.float32)
    _, ys = lax.scan(step, S0, xs)
    return jnp.moveaxis(ys, 0, 1)

def rwkv7_branch(p, mu, w0, w_lora_up, a0, a_lora_up, g_lora_up, k_k, k_a, r_k, ln_w, ln_b):
    Bsz, T, _ = p.shape
    f32 = jnp.float32
    p = p + (token_shift(p) - p) * mu
    r, k, v, xw, xa, xg = jnp.split(
        p, [RWKV_WIDTH, 2 * RWKV_WIDTH, 3 * RWKV_WIDTH,
            3 * RWKV_WIDTH + DECAY_LORA, 3 * RWKV_WIDTH + DECAY_LORA + ICLR_LORA], axis=-1)
    w_log = -jax.nn.softplus(-(w0 + jnp.tanh(xw) @ w_lora_up)) - 0.5
    decay = jnp.exp(-jnp.exp(w_log.astype(f32)))
    a = jax.nn.sigmoid(a0 + xa @ a_lora_up)
    g = jax.nn.sigmoid(xg) @ g_lora_up

    def heads(t):
        return t.reshape(Bsz, T, RWKV_HEADS, HEAD_DIM).astype(f32)

    r, k, v, decay, a = heads(r), heads(k), heads(v), heads(decay), heads(a)
    k_k = k_k.reshape(RWKV_HEADS, HEAD_DIM).astype(f32)
    k_a = k_a.reshape(RWKV_HEADS, HEAD_DIM).astype(f32)
    kk = k * k_k
    kk = kk / jnp.maximum(jnp.sqrt(jnp.sum(kk * kk, axis=-1, keepdims=True)), 1e-12)
    k = k * (1.0 + (a - 1.0) * k_a)
    y = wkv7_scan(r, decay, k, v, -kk, kk * a)
    mean = jnp.mean(y, axis=-1, keepdims=True)
    var = jnp.mean(jnp.square(y - mean), axis=-1, keepdims=True)
    y = (y - mean) * lax.rsqrt(var + GN_EPS)
    y = y * ln_w.reshape(RWKV_HEADS, HEAD_DIM).astype(f32) + ln_b.reshape(RWKV_HEADS, HEAD_DIM).astype(f32)
    bonus = jnp.sum(r * k * r_k.astype(f32), axis=-1, keepdims=True) * v
    y = (y + bonus).reshape(Bsz, T, RWKV_WIDTH) * g.astype(f32)
    return y.astype(p.dtype)

def sliding_window_attention(q, k, v, sinks):
    Bsz, T = q.shape[:2]
    nb = T // BLOCK
    f32 = jnp.float32
    qb = q.reshape(Bsz, nb, BLOCK, ATT_KV_HEADS, ATT_GROUP, HEAD_DIM)

    def with_prev(t):
        tb = t.reshape(Bsz, nb, BLOCK, ATT_KV_HEADS, HEAD_DIM)
        prev = jnp.pad(tb, ((0, 0), (1, 0), (0, 0), (0, 0), (0, 0)))[:, :-1]
        return jnp.concatenate([prev, tb], axis=2)

    kc, vc = with_prev(k), with_prev(v)
    scale = HEAD_DIM ** -0.5
    s = jnp.einsum('bnqhgd,bnkhd->bnhgqk', qb, kc).astype(f32) * scale
    qi = jnp.arange(BLOCK)[:, None]
    kj = jnp.arange(2 * BLOCK)[None, :]
    band = (kj <= qi + BLOCK) & (kj > qi + BLOCK - WINDOW)
    valid = (jnp.arange(nb)[:, None, None] > 0) | (kj >= BLOCK)[None]
    mask = (band[None] & valid)[None, :, None, None]
    s = jnp.where(mask, s, -jnp.inf)
    sink = sinks.astype(f32).reshape(1, 1, ATT_KV_HEADS, ATT_GROUP, 1, 1)
    m = jnp.maximum(jnp.max(s, axis=-1, keepdims=True), sink)
    pexp = jnp.exp(s - m)
    denom = jnp.sum(pexp, axis=-1, keepdims=True) + jnp.exp(sink - m)
    probs = (pexp / denom).astype(v.dtype)
    o = jnp.einsum('bnhgqk,bnkhd->bnqhgd', probs, vc)
    return o.reshape(Bsz, T, ATT_WIDTH)

def attention_branch(p, q_norm, k_norm, sinks):
    Bsz, T, _ = p.shape
    q, k, v = jnp.split(p, [ATT_WIDTH, ATT_WIDTH + KV_WIDTH], axis=-1)
    q = rms_norm_2(q.reshape(Bsz, T, ATT_Q_HEADS, HEAD_DIM), q_norm)
    k = rms_norm_2(k.reshape(Bsz, T, ATT_KV_HEADS, HEAD_DIM), k_norm)
    v = v.reshape(Bsz, T, ATT_KV_HEADS, HEAD_DIM)
    return sliding_window_attention(q, k, v, sinks)

def second_inputs(seed: int = 0) -> dict:
    key = jax.random.key(seed)
    ks = iter(jax.random.split(key, 40))
    L = DEPTH_2

    def nrm(shape, scale):
        return jax.random.normal(next(ks), shape, jnp.float32) * scale

    def gain(shape):
        return 1.0 + nrm(shape, 0.02)

    return {
        "x": jax.random.normal(next(ks), (BATCH, SEQ, D_MODEL), jnp.float32),
        "ffn1_norm": gain((L, D_MODEL)),
        "ffn1_w_gate": nrm((L, D_MODEL, D_FF_2), D_MODEL ** -0.5),
        "ffn1_w_up": nrm((L, D_MODEL, D_FF_2), D_MODEL ** -0.5),
        "ffn1_w_down": nrm((L, D_FF_2, D_MODEL), D_FF_2 ** -0.5),
        "mix_norm": gain((L, D_MODEL)),
        "w_in": nrm((L, D_MODEL, IN_COLS), D_MODEL ** -0.5),
        "rwkv_mu": jax.random.uniform(next(ks), (L, RWKV_COLS), jnp.float32),
        "rwkv_w0": jax.random.uniform(next(ks), (L, RWKV_WIDTH), jnp.float32, -6.5, -1.5),
        "rwkv_w_lora_up": nrm((L, DECAY_LORA, RWKV_WIDTH), 0.1),
        "rwkv_a0": nrm((L, RWKV_WIDTH), 0.1),
        "rwkv_a_lora_up": nrm((L, ICLR_LORA, RWKV_WIDTH), 0.1),
        "rwkv_g_lora_up": nrm((L, GATE_LORA, RWKV_WIDTH), GATE_LORA ** -0.5),
        "rwkv_k_k": 0.85 + nrm((L, RWKV_WIDTH), 0.02),
        "rwkv_k_a": gain((L, RWKV_WIDTH)),
        "rwkv_r_k": nrm((L, RWKV_HEADS, HEAD_DIM), 0.1),
        "rwkv_ln_w": gain((L, RWKV_WIDTH)),
        "rwkv_ln_b": nrm((L, RWKV_WIDTH), 0.02),
        "attn_q_norm": gain((L, HEAD_DIM)),
        "attn_k_norm": gain((L, HEAD_DIM)),
        "attn_sinks": nrm((L, ATT_Q_HEADS), 0.5),
        "w_branch_rwkv": nrm((L, RWKV_WIDTH, D_MODEL), RWKV_WIDTH ** -0.5),
        "w_branch_attn": nrm((L, ATT_WIDTH, D_MODEL), ATT_WIDTH ** -0.5),
        "w_out": nrm((L, D_MODEL, D_MODEL), D_MODEL ** -0.5),
        "ffn2_norm": gain((L, D_MODEL)),
        "ffn2_w_gate": nrm((L, D_MODEL, D_FF_2), D_MODEL ** -0.5),
        "ffn2_w_up": nrm((L, D_MODEL, D_FF_2), D_MODEL ** -0.5),
        "ffn2_w_down": nrm((L, D_FF_2, D_MODEL), D_FF_2 ** -0.5),
        "final_norm": gain((L, D_MODEL)),
    }

def second_block(x, ffn1_norm, ffn1_w_gate, ffn1_w_up, ffn1_w_down, mix_norm, w_in,
              rwkv_mu, rwkv_w0, rwkv_w_lora_up, rwkv_a0, rwkv_a_lora_up, rwkv_g_lora_up,
              rwkv_k_k, rwkv_k_a, rwkv_r_k, rwkv_ln_w, rwkv_ln_b,
              attn_q_norm, attn_k_norm, attn_sinks,
              w_branch_rwkv, w_branch_attn, w_out,
              ffn2_norm, ffn2_w_gate, ffn2_w_up, ffn2_w_down, final_norm):
    for l in range(DEPTH_2):
        x = x + 0.5 * swiglu(rms_norm_2(x, ffn1_norm[l]), ffn1_w_gate[l], ffn1_w_up[l], ffn1_w_down[l])
        h = rms_norm_2(x, mix_norm[l])
        proj = h @ w_in[l]
        p_rwkv, p_att, p_gate = jnp.split(proj, [RWKV_COLS, RWKV_COLS + ATT_COLS], axis=-1)
        y_rwkv = rwkv7_branch(p_rwkv, rwkv_mu[l], rwkv_w0[l], rwkv_w_lora_up[l], rwkv_a0[l],
                              rwkv_a_lora_up[l], rwkv_g_lora_up[l], rwkv_k_k[l], rwkv_k_a[l],
                              rwkv_r_k[l], rwkv_ln_w[l], rwkv_ln_b[l])
        y_att = attention_branch(p_att, attn_q_norm[l], attn_k_norm[l], attn_sinks[l])
        gate_rwkv, gate_att = jnp.split(jax.nn.sigmoid(p_gate), N_BRANCH, axis=-1)
        merged = gate_rwkv * (y_rwkv @ w_branch_rwkv[l]) + gate_att * (y_att @ w_branch_attn[l])
        x = x + merged @ w_out[l]
        x = x + 0.5 * swiglu(rms_norm_2(x, ffn2_norm[l]), ffn2_w_gate[l], ffn2_w_up[l], ffn2_w_down[l])
        x = rms_norm_2(x, final_norm[l])
    return x


_first_inputs = second_inputs


def second_inputs(seed=0):
    import zlib

    import numpy as np

    out = dict(_first_inputs(seed))
    spreads = {}
    factors = {'ffn1_norm': 5.655,
     'mix_norm': 4.814,
     'rwkv_w_lora_up': 23.093,
     'rwkv_a0': 4.9,
     'rwkv_k_k': 64.0,
     'rwkv_k_a': 8.0,
     'rwkv_ln_w': 64.0,
     'rwkv_ln_b': 64.0,
     'attn_q_norm': 64.0,
     'attn_k_norm': 64.0,
     'attn_sinks': 64.0,
     'ffn2_norm': 53.988,
     'final_norm': 7.512,
     'rwkv_w0': 3.272}
    for name, (base, spread) in spreads.items():
        noise = np.random.default_rng([zlib.crc32(name.encode()), seed]).standard_normal(out[name].shape)
        drawn = base * np.exp(spread * noise) if base else spread * noise
        out[name] = __import__('jax').numpy.asarray(drawn.astype(out[name].dtype))
    for name, factor in factors.items():
        out[name] = (out[name] * factor).astype(out[name].dtype)
    return out


_narrow_inputs = second_inputs


def second_inputs(seed=0):

    out = dict(_narrow_inputs(seed))
    wider = {'rwkv_k_k': 11.37,
     'rwkv_ln_w': 6.35,
     'rwkv_ln_b': 6.56,
     'attn_q_norm': 5.32,
     'attn_k_norm': 5.4,
     'final_norm': 3.09}
    for name, times in wider.items():
        mean = out[name].mean()
        out[name] = (mean + times * (out[name] - mean)).astype(out[name].dtype)
    return out


DEPTH_3 = 1

CHUNK = 64
SB_HEADS = 8
SB_HEAD_DIM = 64
SB_WIDTH = SB_HEADS * SB_HEAD_DIM
SSM_WIDTH = D_MODEL // 2
SSM_GROUP = 16
SSM_GROUPS = SSM_WIDTH // SSM_GROUP
SSM_STATE = 64
DT_MIN = 1e-3
DT_MAX = 1e-1
FFN_HIDDEN = ((8 * D_MODEL // 3 + 255) // 256) * 256
IN_SPLITS = (SB_WIDTH, 2 * SB_WIDTH, 3 * SB_WIDTH, 3 * SB_WIDTH + SSM_WIDTH,
             3 * SB_WIDTH + SSM_WIDTH + D_MODEL)
IN_COLS_3 = 3 * SB_WIDTH + SSM_WIDTH + 2 * D_MODEL
N_MOD = 6
DEEPNORM_ALPHA = (2 * DEPTH_3) ** 0.25
DEEPNORM_BETA = (8 * DEPTH_3) ** -0.25
LN_EPS = 1e-5


def _normalize(x):
    xf = x.astype(jnp.float32)
    mu = jnp.mean(xf, axis=-1, keepdims=True)
    var = jnp.mean(jnp.square(xf - mu), axis=-1, keepdims=True)
    return ((xf - mu) * lax.rsqrt(var + LN_EPS)).astype(x.dtype)

def _layer_norm(x, g, b):
    return _normalize(x) * g + b

def stick_breaking_attention(q, k, v):
    b, s, h, dh = q.shape
    nb = s // Q_BLOCK
    f32 = jnp.float32
    qb = q.astype(f32).reshape(b, nb, Q_BLOCK, h, dh).transpose(1, 0, 3, 2, 4)
    kt = k.astype(f32).transpose(0, 2, 1, 3)
    vt = v.astype(f32).transpose(0, 2, 1, 3)
    key_pos = jnp.arange(s, dtype=jnp.int32)
    scale = 1.0 / math.sqrt(dh)

    def one_block(args):
        q_blk, blk = args
        q_pos = blk * Q_BLOCK + jnp.arange(Q_BLOCK, dtype=jnp.int32)
        z = jnp.einsum('bhqd,bhkd->bhqk', q_blk, kt) * scale
        causal = key_pos[None, :] < q_pos[:, None]
        log_beta = jax.nn.log_sigmoid(z)
        log_one_minus = jnp.where(causal, log_beta - z, 0.0)
        after = lax.cumsum(log_one_minus, axis=3, reverse=True) - log_one_minus
        w = jnp.where(causal, jnp.exp(log_beta + after), 0.0)
        return jnp.einsum('bhqk,bhkd->bhqd', w, vt)

    out = lax.map(one_block, (qb, jnp.arange(nb, dtype=jnp.int32)))
    return out.transpose(1, 0, 3, 2, 4).reshape(b, s, h * dh).astype(v.dtype)

def s5_branch(u, a_re, a_im, log_dt, b_re, b_im, c_re, c_im, d_skip, w_glu, b_glu):
    f32 = jnp.float32
    c64 = jnp.complex64
    bsz, s, _ = u.shape
    n_chunks = s // CHUNK
    uf = u.astype(f32)
    lam = lax.complex(a_re.astype(f32), a_im.astype(f32))
    dt = jnp.exp(log_dt.astype(f32))[:, None]
    lam_dt = lam * dt
    lam_bar = jnp.exp(lam_dt)
    b_mat = lax.complex(b_re.astype(f32), b_im.astype(f32))
    b_bar = ((lam_bar - 1.0) / lam)[..., None] * b_mat
    c_mat = lax.complex(c_re.astype(f32), c_im.astype(f32))
    steps = jnp.arange(1, CHUNK + 1, dtype=f32)
    powers = jnp.exp(lam_dt[None] * steps[:, None, None].astype(c64))
    a_seq = jnp.broadcast_to(lam_bar[None, None], (CHUNK, bsz, SSM_GROUPS, SSM_STATE))

    u_chunks = uf.reshape(bsz, n_chunks, CHUNK, SSM_GROUPS, SSM_GROUP).transpose(1, 2, 0, 3, 4)

    def combine(left, right):
        a_l, b_l = left
        a_r, b_r = right
        return a_r * a_l, a_r * b_l + b_r

    def step(state, u_c):
        bu = jnp.einsum('gpc,lbgc->lbgp', b_bar, u_c.astype(c64))
        _, h_loc = lax.associative_scan(combine, (a_seq, bu), axis=0)
        h = h_loc + powers[:, None] * state[None]
        y = jnp.einsum('gcp,lbgp->lbgc', c_mat, h).real
        return h[-1], y

    state0 = jnp.zeros((bsz, SSM_GROUPS, SSM_STATE), c64)
    _, ys = lax.scan(step, state0, u_chunks)
    y = ys.transpose(2, 0, 1, 3, 4).reshape(bsz, s, SSM_WIDTH)
    y = y + d_skip.astype(f32) * uf
    y = jax.nn.gelu(y)
    y = y * jax.nn.sigmoid(y @ w_glu.astype(f32) + b_glu.astype(f32))
    return y.astype(u.dtype)

def token_mixer(h, w_in, w_sb_up, a_re, a_im, log_dt, b_re, b_im, c_re, c_im,
                d_skip, w_glu, b_glu, w_ssm_up, w_out):
    bsz, s, _ = h.shape
    proj = h @ w_in
    q, k, v, u, g_sb, g_ssm = jnp.split(proj, IN_SPLITS, axis=-1)
    shp = (bsz, s, SB_HEADS, SB_HEAD_DIM)
    y_sb = stick_breaking_attention(q.reshape(shp), k.reshape(shp), v.reshape(shp)) @ w_sb_up
    y_ssm = s5_branch(u, a_re, a_im, log_dt, b_re, b_im, c_re, c_im,
                      d_skip, w_glu, b_glu) @ w_ssm_up
    merged = jax.nn.sigmoid(g_sb) * y_sb + jax.nn.sigmoid(g_ssm) * y_ssm
    return merged @ w_out

def swiglu_ffn(h, w_ffn_in, w_ffn_out):
    gate, up = jnp.split(h @ w_ffn_in, 2, axis=-1)
    return (jax.nn.silu(gate) * up) @ w_ffn_out

def third_inputs(seed: int = 0) -> dict:
    key = jax.random.key(seed)
    ks = jax.random.split(key, 32)
    f32 = jnp.float32

    def nrm(k, shape, scale):
        return jax.random.normal(k, shape, f32) * scale

    G, P, Cg = SSM_GROUPS, SSM_STATE, SSM_GROUP
    n = jnp.arange(P, dtype=f32)
    return {
        "x": nrm(ks[0], (BATCH, SEQ, D_MODEL), 1.0),
        "c": nrm(ks[1], (BATCH, D_MODEL), 1.0),
        "w_ada": nrm(ks[2], (DEPTH_3, D_MODEL, N_MOD * D_MODEL), 0.5 * D_MODEL ** -0.5),
        "b_ada": nrm(ks[3], (DEPTH_3, N_MOD * D_MODEL), 0.02),
        "w_in": nrm(ks[4], (DEPTH_3, D_MODEL, IN_COLS_3), D_MODEL ** -0.5),
        "w_sb_up": nrm(ks[5], (DEPTH_3, SB_WIDTH, D_MODEL), SB_WIDTH ** -0.5),
        "ssm_a_re": -0.5 + nrm(ks[6], (DEPTH_3, G, P), 0.01),
        "ssm_a_im": math.pi * n + nrm(ks[7], (DEPTH_3, G, P), 0.01),
        "ssm_log_dt": jax.random.uniform(ks[8], (DEPTH_3, G), f32,
                                         math.log(DT_MIN), math.log(DT_MAX)),
        "ssm_b_re": nrm(ks[9], (DEPTH_3, G, P, Cg), (2 * Cg) ** -0.5),
        "ssm_b_im": nrm(ks[10], (DEPTH_3, G, P, Cg), (2 * Cg) ** -0.5),
        "ssm_c_re": nrm(ks[11], (DEPTH_3, G, Cg, P), P ** -0.5),
        "ssm_c_im": nrm(ks[12], (DEPTH_3, G, Cg, P), P ** -0.5),
        "ssm_d": 1.0 + nrm(ks[13], (DEPTH_3, SSM_WIDTH), 0.1),
        "w_glu": nrm(ks[14], (DEPTH_3, SSM_WIDTH, SSM_WIDTH), SSM_WIDTH ** -0.5),
        "b_glu": nrm(ks[15], (DEPTH_3, SSM_WIDTH), 0.02),
        "w_ssm_up": nrm(ks[16], (DEPTH_3, SSM_WIDTH, D_MODEL), SSM_WIDTH ** -0.5),
        "w_out": nrm(ks[17], (DEPTH_3, D_MODEL, D_MODEL), D_MODEL ** -0.5 * DEEPNORM_BETA),
        "ln1_g": 1.0 + nrm(ks[18], (DEPTH_3, D_MODEL), 0.02),
        "ln1_b": nrm(ks[19], (DEPTH_3, D_MODEL), 0.02),
        "w_ffn_in": nrm(ks[20], (DEPTH_3, D_MODEL, 2 * FFN_HIDDEN), D_MODEL ** -0.5),
        "w_ffn_out": nrm(ks[21], (DEPTH_3, FFN_HIDDEN, D_MODEL), FFN_HIDDEN ** -0.5 * DEEPNORM_BETA),
        "ln2_g": 1.0 + nrm(ks[22], (DEPTH_3, D_MODEL), 0.02),
        "ln2_b": nrm(ks[23], (DEPTH_3, D_MODEL), 0.02),
    }

def third_block(x, c, w_ada, b_ada, w_in, w_sb_up, ssm_a_re, ssm_a_im, ssm_log_dt,
              ssm_b_re, ssm_b_im, ssm_c_re, ssm_c_im, ssm_d, w_glu, b_glu,
              w_ssm_up, w_out, ln1_g, ln1_b, w_ffn_in, w_ffn_out, ln2_g, ln2_b):
    c_act = jax.nn.silu(c)
    for l in range(DEPTH_3):
        mod = c_act @ w_ada[l] + b_ada[l]
        sh_m, sc_m, g_m, sh_f, sc_f, g_f = [m[:, None, :] for m in jnp.split(mod, N_MOD, axis=-1)]
        h = _normalize(x) * (1.0 + sc_m) + sh_m
        y = token_mixer(h, w_in[l], w_sb_up[l], ssm_a_re[l], ssm_a_im[l], ssm_log_dt[l],
                        ssm_b_re[l], ssm_b_im[l], ssm_c_re[l], ssm_c_im[l], ssm_d[l],
                        w_glu[l], b_glu[l], w_ssm_up[l], w_out[l])
        x = _layer_norm(DEEPNORM_ALPHA * x + (1.0 + g_m) * y, ln1_g[l], ln1_b[l])
        h = _normalize(x) * (1.0 + sc_f) + sh_f
        y = swiglu_ffn(h, w_ffn_in[l], w_ffn_out[l])
        x = _layer_norm(DEEPNORM_ALPHA * x + (1.0 + g_f) * y, ln2_g[l], ln2_b[l])
    return x


_first_inputs_3 = third_inputs


def third_inputs(seed=0):
    import zlib

    import numpy as np

    out = dict(_first_inputs_3(seed))
    spreads = {}
    factors = {'b_ada': 3.236,
     'ssm_a_re': 64.0,
     'ssm_a_im': 43.608,
     'ssm_log_dt': 47.528,
     'ssm_b_re': 61.256,
     'ssm_b_im': 61.48,
     'ssm_c_re': 58.856,
     'ssm_c_im': 58.608,
     'ssm_d': 4.351,
     'b_glu': 24.702,
     'ln1_g': 8.007,
     'ln1_b': 7.846,
     'ln2_g': 7.895,
     'ln2_b': 8.189}
    for name, (base, spread) in spreads.items():
        noise = np.random.default_rng([zlib.crc32(name.encode()), seed]).standard_normal(out[name].shape)
        drawn = base * np.exp(spread * noise) if base else spread * noise
        out[name] = __import__('jax').numpy.asarray(drawn.astype(out[name].dtype))
    for name, factor in factors.items():
        out[name] = (out[name] * factor).astype(out[name].dtype)
    return out


_narrow_inputs_3 = third_inputs


def third_inputs(seed=0):

    out = dict(_narrow_inputs_3(seed))
    wider = {'ln1_g': 3.26, 'ln1_b': 3.26, 'ln2_g': 3.16, 'ln2_b': 3.16}
    for name, times in wider.items():
        mean = out[name].mean()
        out[name] = (mean + times * (out[name] - mean)).astype(out[name].dtype)
    return out


def setup_inputs(seed=0):
    out = dict(first_inputs(seed))
    for name, value in second_inputs(seed + 1).items():
        if name != "x":
            out[name + "_2"] = value
    for name, value in third_inputs(seed + 2).items():
        if name != "x":
            out[name + "_3"] = value
    return out


def reference(
    x, mem, norm_mix_g, norm_mlp_g, mem_norm_g, w_mem_kv, mem_q_norm_g, mem_k_norm_g, w_out,
    w_mlp_in, w_mlp_out, a_w_in, a_b_glu, a_dw, a_dw_b, a_ln_g, a_ln_b, b_w_in, b_gate_b,
    b_q_norm_g, kv_norm_g, w_kv, k_norm_g, cmp_pe_k, cmp_pe_v, cmp_w1_k, cmp_w2_k, cmp_w1_v,
    cmp_w2_v, ffn1_norm_2, ffn1_w_gate_2, ffn1_w_up_2, ffn1_w_down_2, mix_norm_2, w_in_2,
    rwkv_mu_2, rwkv_w0_2, rwkv_w_lora_up_2, rwkv_a0_2, rwkv_a_lora_up_2, rwkv_g_lora_up_2,
    rwkv_k_k_2, rwkv_k_a_2, rwkv_r_k_2, rwkv_ln_w_2, rwkv_ln_b_2, attn_q_norm_2, attn_k_norm_2,
    attn_sinks_2, w_branch_rwkv_2, w_branch_attn_2, w_out_2, ffn2_norm_2, ffn2_w_gate_2,
    ffn2_w_up_2, ffn2_w_down_2, final_norm_2, c_3, w_ada_3, b_ada_3, w_in_3, w_sb_up_3,
    ssm_a_re_3, ssm_a_im_3, ssm_log_dt_3, ssm_b_re_3, ssm_b_im_3, ssm_c_re_3, ssm_c_im_3,
    ssm_d_3, w_glu_3, b_glu_3, w_ssm_up_3, w_out_3, ln1_g_3, ln1_b_3, w_ffn_in_3, w_ffn_out_3,
    ln2_g_3, ln2_b_3,
):
    x = first_block(
        x, mem, norm_mix_g, norm_mlp_g, mem_norm_g, w_mem_kv, mem_q_norm_g, mem_k_norm_g, w_out,
        w_mlp_in, w_mlp_out, a_w_in, a_b_glu, a_dw, a_dw_b, a_ln_g, a_ln_b, b_w_in, b_gate_b,
        b_q_norm_g, kv_norm_g, w_kv, k_norm_g, cmp_pe_k, cmp_pe_v, cmp_w1_k, cmp_w2_k, cmp_w1_v,
        cmp_w2_v,
    )
    x = second_block(
        x, ffn1_norm_2, ffn1_w_gate_2, ffn1_w_up_2, ffn1_w_down_2, mix_norm_2, w_in_2,
        rwkv_mu_2, rwkv_w0_2, rwkv_w_lora_up_2, rwkv_a0_2, rwkv_a_lora_up_2, rwkv_g_lora_up_2,
        rwkv_k_k_2, rwkv_k_a_2, rwkv_r_k_2, rwkv_ln_w_2, rwkv_ln_b_2, attn_q_norm_2,
        attn_k_norm_2, attn_sinks_2, w_branch_rwkv_2, w_branch_attn_2, w_out_2, ffn2_norm_2,
        ffn2_w_gate_2, ffn2_w_up_2, ffn2_w_down_2, final_norm_2,
    )
    return third_block(
        x, c_3, w_ada_3, b_ada_3, w_in_3, w_sb_up_3, ssm_a_re_3, ssm_a_im_3, ssm_log_dt_3,
        ssm_b_re_3, ssm_b_im_3, ssm_c_re_3, ssm_c_im_3, ssm_d_3, w_glu_3, b_glu_3, w_ssm_up_3,
        w_out_3, ln1_g_3, ln1_b_3, w_ffn_in_3, w_ffn_out_3, ln2_g_3, ln2_b_3,
    )


_drawn_inputs = setup_inputs


def setup_inputs(seed=0):
    import zlib

    import numpy as np

    out = dict(_drawn_inputs(seed))
    spreads = {}
    factors = {'b_gate_b': 8.0, 'cmp_pe_k': 3.62, 'b_ada_3': 4.495, 'ssm_d_3': 5.839, 'b_glu_3': 6.192}
    for name, (base, spread) in spreads.items():
        noise = np.random.default_rng([zlib.crc32(name.encode()), seed]).standard_normal(out[name].shape)
        drawn = base * np.exp(spread * noise) if base else spread * noise
        out[name] = __import__('jax').numpy.asarray(drawn.astype(out[name].dtype))
    for name, factor in factors.items():
        out[name] = (out[name] * factor).astype(out[name].dtype)
    return out
```

```python
from contextlib import ExitStack

import numpy as np
import concourse.bass as bass
from concourse import mybir

F = mybir.dt.float32
R = mybir.dt.float32r
ALU = mybir.AluOpType
ACT = mybir.ActivationFunctionType
AX = mybir.AxisListType


class Queue:

    def __init__(self, name, sem, chained):
        self.name, self.sem, self.chained = name, sem, chained
        self.items, self.count, self.seen = [], 0, {}

    def wait(self, *toks):
        for t in toks:
            if t is None:
                continue
            sem, v = t
            if self.seen.get(id(sem), 0) < v:
                self.seen[id(sem)] = v
                self.items.append((None, sem, v))

    def op(self, fn, *toks, inc=True):
        self.wait(*toks)
        if self.chained and self.count:
            self.wait((self.sem, self.count))
        if inc:
            self.count += 1
            self.items.append((fn, self.sem, 1))
        else:
            self.items.append((fn, None, 0))
        return self.tok()

    def dma(self, fn, sem, *toks):
        self.wait(*toks)
        self.items.append((fn, sem, 16))

    def tok(self):
        return (self.sem, self.count)

    def emit(self, eng):
        for fn, sem, v in self.items:
            if fn is None:
                eng.wait_ge(sem, v)
            else:
                ins = fn(eng)
                if sem is not None:
                    ins.then_inc(sem, v)


class Banks:

    def __init__(self, tiles):
        self.tiles = tiles
        self.free = [(i, None) for i in range(len(tiles))]

    def take(self):
        i, tok = self.free.pop(0)
        return i, self.tiles[i], tok

    def give(self, i, tok):
        self.free.append((i, tok))


class Ring:

    def __init__(self, n):
        self.n, self.i, self.toks = n, -1, [() for _ in range(n)]

    def next(self):
        self.i = (self.i + 1) % self.n
        return self.i, self.toks[self.i]

    def done(self, i, *toks):
        self.toks[i] = toks


class K:

    NRAW, NSPL = 3, 3

    def __init__(self, nc, ctx):
        self.nc, self.ctx = nc, ctx
        self.n = 0
        sem = self.sem
        self.pe = Queue("tensor", sem("q_pe"), False)
        self.act = Queue("scalar", sem("q_act"), True)
        self.dve = Queue("vector", sem("q_dve"), True)
        self.pool = Queue("gpsimd", sem("q_pool"), True)
        self.sp = Queue("sync", sem("q_sp"), False)
        self.ps = Banks([ctx.enter_context(nc.psum_tensor(f"bank{i}", [128, 512], F)) for i in range(8)])
        self.raw = [self.sb(f"raw{i}", [128, 2048]) for i in range(self.NRAW)]
        self.w_base = -(-self.nc.sbuf_base // 32) * 32
        self.whi = [self.sb(f"whi{i}", [128, 2048], R) for i in range(self.NSPL)]
        self.wlo = [self.sb(f"wlo{i}", [128, 2048], R) for i in range(self.NSPL)]
        self.raw_sem = [sem(f"s_raw{i}") for i in range(self.NRAW)]
        self.raw_cnt = [0] * self.NRAW
        self.raw_ring, self.spl_ring = Ring(self.NRAW), Ring(self.NSPL)

    def sem(self, name):
        return self.ctx.enter_context(self.nc.semaphore(name))

    def sb(self, name, shape, dt=F, ctx=None):
        self.n += 1
        return (ctx or self.ctx).enter_context(self.nc.sbuf_tensor(f"{name}_{self.n}", shape, dt))

    def borrow(self, shapes):
        out, o = {}, 0
        for n, shape in shapes.items():
            self.n += 1
            out[n] = self.nc.alloc_sbuf_tensor_at(f"{n}_{self.n}", [128, *shape], F,
                                                       offset=self.w_base + o)
            o += -(-4 * int(np.prod(shape)) // 32) * 32
        assert o <= 2 * self.NSPL * 8192
        for toks in self.spl_ring.toks:
            for q in (self.pe, self.act, self.dve):
                q.wait(*toks)
        return out

    def give_back(self, *toks):
        for i in range(self.NSPL):
            self.spl_ring.done(i, *toks)

    def barrier(self):
        toks = [q.tok() for q in (self.pe, self.act, self.dve)]
        for q in (self.pe, self.act, self.dve):
            q.wait(*toks)

    def load(self, pieces):
        i, toks = self.raw_ring.next()
        for dst, src in pieces(self.raw[i]):
            self.sp.dma(lambda e, d=dst, s=src: e.dma_start(d, s), self.raw_sem[i], *toks)
            self.raw_cnt[i] += 16
        return i, (self.raw_sem[i], self.raw_cnt[i])

    def slab_raw(self, W, r0, kt, c0, nw):
        def pieces(raw):
            v = raw[:, 0:kt * nw].rearrange("p (k n) -> p k n", k=kt)
            return [(v, W[r0:r0 + kt * 128, c0:c0 + nw].rearrange("(k p) n -> p k n", p=128))]
        i, tok = self.load(pieces)
        return i, self.raw[i][:, 0:kt * nw].rearrange("p (k n) -> p k n", k=kt), tok

    def slab(self, W, r0, kt, c0, nw):
        i, _, landed = self.slab_raw(W, r0, kt, c0, nw)
        j, free = self.spl_ring.next()
        m = kt * nw
        raw, hi, lo = self.raw[i], self.whi[j], self.wlo[j]
        self.pool.op(lambda e: e.tensor_scalar(hi[:, 0:m], raw[:, 0:m], 1.0, 0.0, ALU.mult, ALU.add), landed, *free)
        t = self.pool.op(lambda e: e.tensor_tensor(lo[:, 0:m], raw[:, 0:m], hi[:, 0:m].bitcast(F), ALU.subtract))
        self.raw_ring.done(i, t)
        sh = hi[:, 0:m].rearrange("p (k n) -> p k n", k=kt)
        sl = lo[:, 0:m].rearrange("p (k n) -> p k n", k=kt)
        return j, sh, sl, t

    def mm(self, out, lhsT, rhs, start, stop, *toks, inc=False):
        return self.pe.op(lambda e: e.matmul(out, lhsT, rhs, start=start, stop=stop), *toks, inc=inc)

    def mma(self, out, lhsT, rhs, start, stop, *toks, inc=False):
        return self.pe.op(lambda e: e.matmul(out, lhsT, rhs, start=start, stop=stop, skip_group_check=True),
                          *toks, inc=inc)

    def tr(self, out, src, ident, *toks, inc=False):
        return self.pe.op(lambda e: e.transpose(out, src, ident), *toks, inc=inc)

    @staticmethod
    def parts(toks, k):
        return tuple(t[k] if isinstance(t, list) else t for t in toks if k == 0 or isinstance(t, list))

    def lin(self, W, r0, kt, tiles, act, evac, *toks):
        per = 2048 // (kt * 128) if kt in (1, 2, 4, 8) else 2
        n = 0
        while n < len(tiles):
            m = 1
            while m < per and n + m < len(tiles) and tiles[n + m] == tiles[n] + 128 * m:
                m += 1
            j, hi, lo, ready = self.slab(W, r0, kt, tiles[n], 128 * m)
            together = n == 0 and any(isinstance(t, list) for t in toks)
            for run in ([list(range(m))] if together else [[i] for i in range(m)]):
                banks, done = [self.ps.take() for _ in run], []
                for k in range(kt):
                    ah, al = act(k)
                    for i, (b, bank, free) in zip(run, banks):
                        s = slice(128 * i, 128 * i + 128)
                        w = ((ready, free) if k == 0 else ()) + self.parts(toks, k)
                        self.mma(bank[:, :], hi[:, k, s], ah, k == 0, False, *w)
                        self.mma(bank[:, :], hi[:, k, s], al, False, False)
                        t = self.mma(bank[:, :], lo[:, k, s], ah, False, k == kt - 1, inc=(k == kt - 1))
                        if k == kt - 1:
                            done.append(t)
                for i, (b, bank, _), t in zip(run, banks, done):
                    evac(n + i, b, bank, t)
            self.spl_ring.done(j, self.pe.tok())
            n += m

    def lin_tok(self, W, r0, kt, c0, nw, act, nt, evac, *toks):
        banks = [self.ps.take() for _ in range(nt)]
        step = 2048 // nw
        step = min(step, kt)
        for k0 in range(0, kt, step):
            j, hi, lo, ready = self.slab(W, r0 + 128 * k0, step, c0, nw)
            together = k0 + step < kt and any(isinstance(t, list) for t in toks)
            order = [(k, t) for k in range(step) for t in range(nt)] if together else \
                [(k, t) for t in range(nt) for k in range(step)]
            for k, t in order:
                b, bank, free = banks[t]
                ah, al = act(k0 + k, t)
                w = ((ready, free) if k == 0 else ()) + self.parts(toks, k0 + k)
                first, last = k0 + k == 0, k0 + k == kt - 1
                self.mma(bank[:, 0:nw], ah, hi[:, k, :], first, False, *w)
                self.mma(bank[:, 0:nw], ah, lo[:, k, :], False, False)
                tk = self.mma(bank[:, 0:nw], al, hi[:, k, :], False, last, inc=(k == step - 1))
                if last:
                    evac(t, b, bank, tk)
            self.spl_ring.done(j, self.pe.tok())
class Net(K):

    def setup(self, A):
        self.A = A
        sb, sem = self.sb, self.sem
        self.x = sb("x", [128, 8, 512])
        self.par = sb("par", [128, NPAR])
        self.cst = sb("cst", [128, NCST])
        self.s_in = sem("s_in")
        self.n_in = 0
        self.actdma(self.cst[:, :], A["cst"])
        self.actdma(self.par[:, :], A["par"])
        self.asides, self.behind = [], []
        self.rb_read = self.acc = None
        self.sm = sb("sm", [128, 64])
        self.scr = [sb(f"scr{i}", [128, 512]) for i in range(4)]
        self.scr_ring = Ring(4)
        self.s_scr, self.n_scr = [sem(f"s_scr{i}") for i in range(4)], [0] * 4
        c = self.c
        self.ident, self.ones, self.bones = c("ident"), c("ones"), c("bones")
        self.load_x()

    def load_x(self):
        self.xt = []
        for k in range(8):
            s = self.sem(f"s_x{k}")
            self.act.dma(lambda e, k=k: e.dma_start(self.x[:, k, :], self.A["xT"][128 * k:128 * k + 128, :]), s)
            self.xt.append((s, 16))

    def spend(self, n):
        done = object()
        while n and self.behind:
            if next(self.behind[0], done) is done:
                self.behind.pop(0)
            n -= 1

    def aside(self):
        if self.asides:
            self.asides.pop(0)()

    def acts(self, ctx, n=8):
        self.ah = self.sb("ah", [128, n, 512], R, ctx)
        self.al = self.sb("al", [128, n, 512], R, ctx)

    def actdma(self, dst, src, *toks):
        self.act.dma(lambda e: e.dma_start(dst, src), self.s_in, *toks)
        self.n_in += 16
        return (self.s_in, self.n_in)

    def c(self, name):
        o, n = CST[name]
        return self.cst[:, o:o + n]

    def p(self, name, j=0, n=1):
        o, _ = PAR[name]
        return self.par[:, o + j:o + j + n]

    def ready(self):
        for q in (self.pe, self.act, self.dve):
            q.wait((self.s_in, self.n_in))

    def V(self, fn, *toks):
        return self.dve.op(fn, *toks)

    def S(self, fn, *toks):
        return self.act.op(fn, *toks)

    def tt(self, out, a, b, op, *toks):
        return self.V(lambda e: e.tensor_tensor(out, a, b, op), *toks)

    def ts(self, out, a, s1, s2, op0, op1, *toks):
        if s2 is None:
            return self.V(lambda e: e.tensor_scalar(out, a, s1, None, op0), *toks)
        return self.V(lambda e: e.tensor_scalar(out, a, s1, s2, op0, op1), *toks)

    def stt(self, out, a, s, b, op0, op1, *toks):
        return self.V(lambda e: e.scalar_tensor_tensor(out, a, s, b, op0, op1), *toks)

    def func(self, out, src, f, *toks, bias=None, scale=1.0, accum=None):
        kw = {} if accum is None else {"accum_out": accum}
        if bias is not None:
            kw["bias"] = bias
        return self.S(lambda e: e.activation(out, src, f, scale=scale, **kw), *toks)

    def recip(self, out, src, *toks):
        return self.V(lambda e: e.reciprocal(out, src), *toks)

    def split(self, hi, lo, src, *toks):
        t = self.func(hi, src, ACT.Copy, *toks)
        return self.tt(lo, src, hi.bitcast(F), ALU.subtract, t)

    def sums(self, src, kt, n, *toks, square=True, t_src=None):
        b, bank, free = self.ps.take()
        self.sqrt_table()
        for k in range(kt):
            w = (t_src[k],) if t_src else ()
            if square:
                i, rd = self.scr_ring.next()
                s = self.scr[i][:, 0:n]
                t = self.func(s, src(k), ACT.Square, *w, *toks, *rd)
            else:
                s, t, i = src(k), None, None
            tk = self.mm(bank[:, 0:n], self.ones, s, k == 0, k == kt - 1, free, t, *w, *toks, inc=True)
            if i is not None:
                self.scr_ring.done(i, tk)
        return b, bank, tk

    def sqrt_table(self):
        self.func(self.sm[:, 63:64], self.ones[:, 0:1], ACT.Sqrt)

    def tile_done(self, n, t):
        acc, x = self.rb[:, :], self.x[:, n, :]
        if n == 0:
            self.sqrt_table()
            self.acc = self.func(acc, x, ACT.Square, t, self.rb_read)
        else:
            i, rd = self.scr_ring.next()
            s = self.scr[i][:, :]
            self.acc = self.tt(acc, acc, s, ALU.add, self.func(s, x, ACT.Square, t, *rd), self.acc)
            self.scr_ring.done(i, self.acc)

    def x_squares(self):
        if self.acc is None:
            return self.sums(lambda k: self.x[:, k, :], 8, 512, t_src=self.xt)
        b, bank, free = self.ps.take()
        t = self.mm(bank[:, :], self.ones, self.rb[:, :], True, True, free, self.acc, inc=True)
        self.acc = None
        return b, bank, t

    def rstd(self, out, bank, b, t, n, d, eps):
        t = self.func(out, bank[:, 0:n], ACT.Sqrt, t, self.dve.tok(), scale=1.0 / d, bias=self.c(eps))
        self.ps.give(b, t)
        return self.recip(out, out, t)

    def rms(self, gain, eps="eps6", x=None, kt=8, n=512, t_src=None, again=False):
        own = x is None
        if own:
            x = lambda k: self.x[:, k, :]
        if not again:
            b, bank, t = self.x_squares() if own else self.sums(x, kt, n, t_src=t_src)
            self.rstd(self.rb[:, 0:n], bank, b, t, n, 128.0 * kt, eps)
        return self.split_all(
            kt, n, lambda s, k, *w: self.stt(s, x(k), gain(k), self.rb[:, 0:n], ALU.mult, ALU.mult, *w))

    def split_all(self, kt, n, make, bias=None):
        todo, out = [], []
        free = self.pe.tok()

        def low(k, i, s, t):
            lo, hi = self.al[:, k, 0:n], self.ah[:, k, 0:n].bitcast(F)
            if bias is not None:
                t = self.stt(lo, s, bias(k), hi, ALU.add, ALU.subtract, t, free)
            else:
                t = self.tt(lo, s, hi, ALU.subtract, t, free)
            self.scr_ring.done(i, t)
            out.append(t)
        for k in range(kt):
            i, rd = self.scr_ring.next()
            s = self.scr[i][:, 0:n]
            self.rb_read = t = make(s, k, *rd)
            if bias is None:
                t = self.func(self.ah[:, k, 0:n], s, ACT.Copy, t, free)
            else:
                t = self.func(self.ah[:, k, 0:n], s, ACT.Identity, t, free, bias=bias(k))
            todo.append((k, i, s, t))
            if k:
                low(*todo.pop(0))
        low(*todo.pop(0))
        return out

    def xact(self, k):
        return self.ah[:, k, :], self.al[:, k, :]

    def xact_t(self, k, t):
        s = slice(128 * t, 128 * t + 128)
        return self.ah[:, k, s], self.al[:, k, s]

    def residual(self, W, kt, act, scale, *toks):
        def evac(n, b, bank, t):
            self.xt[n] = t = self.stt(self.x[:, n, :], bank[:, :], scale, self.x[:, n, :], ALU.mult, ALU.add, t)
            self.ps.give(b, t)
            self.tile_done(n, t)
        self.lin(W, 0, kt, [128 * n for n in range(8)], act, evac, *toks)

    def mlp(self, gate_w, W1, W2, dff, add, t_act, squares=True):
        gated = gate_w is not None
        nt = dff // 128
        groups = [list(range(g, min(g + 4, nt))) for g in range(0, nt, 4)]
        with ExitStack() as sc:
            hh = self.sb("hh", [128, 2, 4, 512], R, sc)
            hl = self.sb("hl", [128, 2, 4, 512], R, sc)
            gt = [self.sb("gt", [128, 512], F, sc) for _ in range(4)]
            done = [None, None]
            ready = {}

            def up(g):
                u = g % 2
                tg = {}
                for p0 in range(0, len(groups[g]), 2):
                    pair = groups[g][p0:p0 + 2]

                    def gate(n, b, bank, t, p0=p0):
                        tg[p0 + n] = self.func(gt[p0 + n][:, :], bank[:, :], ACT.Silu, t, self.dve.tok())
                        self.ps.give(b, tg[p0 + n])

                    def value(n, b, bank, t, p0=p0):
                        i, rd = self.scr_ring.next()
                        s = self.scr[i][:, :]
                        if gated:
                            t = self.tt(s, gt[p0 + n][:, :], bank[:, :], ALU.mult, t, tg[p0 + n], *rd)
                            self.ps.give(b, t)
                        else:
                            t = self.func(gt[p0 + n][:, :], bank[:, :], ACT.Relu, t, self.dve.tok())
                            self.ps.give(b, t)
                            t = self.tt(s, gt[p0 + n][:, :], gt[p0 + n][:, :], ALU.mult, t, *rd)
                        t = self.split(hh[:, u, p0 + n, :], hl[:, u, p0 + n, :], s, t, done[u])
                        self.scr_ring.done(i, t)
                        ready[g] = t

                    if gated:
                        self.lin(gate_w[0], 0, 8, [gate_w[1] + 128 * c for c in pair], self.xact, gate, t_act)
                    self.lin(W1[0], 0, 8, [W1[1] + 128 * c for c in pair], self.xact, value, t_act)

            def down(g):
                u = g % 2
                r0 = groups[g][0] * 128

                def evac(n, b, bank, t):
                    self.xt[n] = add(n, bank, t)
                    self.ps.give(b, self.xt[n])
                    if squares and g == len(groups) - 1:
                        self.tile_done(n, self.xt[n])
                self.lin(W2, r0, len(groups[g]), [128 * n for n in range(8)],
                         lambda k: (hh[:, u, k, :], hl[:, u, k, :]), evac, ready[g])
                done[u] = self.pe.tok()

            for g in range(len(groups) + 1):
                if g < len(groups):
                    up(g)
                    self.aside()
                if g:
                    down(g - 1)
                    self.aside()

    def headnorm(self, src, nt, heads, gains, dst, *toks, eps="eps6"):
        w = heads * 64
        with ExitStack() as sc:
            ss = self.sb("ss", [128, nt * heads], F, sc)
            nb = 2 if w <= 512 else 1
            sq = [self.sb("sq", [128, w], F, sc) for _ in range(nb)]
            self.sqrt_table()
            self.act.wait(self.dve.tok())
            rd = [None, None]
            for t in range(nt):
                a = self.func(sq[t % nb][:, :], src(t), ACT.Square, *toks, rd[t % nb])
                o = ss[:, t * heads:(t + 1) * heads]
                i = sq[t % nb][:, :].rearrange("p (h d) -> p h d", d=64)
                rd[t % nb] = self.V(lambda e, o=o, i=i: e.tensor_reduce(o, i, AX.X, ALU.add), a)
            t1 = self.func(ss[:, :], ss[:, :], ACT.Sqrt, rd[0], rd[1], scale=1.0 / 64, bias=self.c(eps))
            self.recip(ss[:, :], ss[:, :], t1)
            for t in range(nt):
                v = src(t).rearrange("p (h d) -> p h d", d=64)
                r = ss[:, t * heads:(t + 1) * heads].unsqueeze(2).to_broadcast([128, heads, 64])
                tk = self.tt(v, v, r, ALU.mult)
            for pr in range(heads // 2):
                self.to_fm(lambda t: src(t)[:, 128 * pr:128 * pr + 128], nt, dst(pr), gains(pr), tk)
            self.barrier()

    def to_fm(self, src, nt, dst, gain, *toks):
        b, bank, free = self.ps.take()
        for t in range(nt):
            tk = self.tr(bank[:, 128 * t:128 * t + 128], src(t), self.ident, free, *toks, inc=(t == nt - 1))
        if gain is None:
            tk = self.func(dst, bank[:, 0:128 * nt], ACT.Copy, tk)
        else:
            tk = self.func(dst, bank[:, 0:128 * nt], ACT.Copy, tk, scale=gain)
        self.ps.give(b, tk)
        return tk

    def softmax_units(self, units, sc):
        NP, NT, NSM = 6, 4, 12
        self.pe.wait(self.dve.tok(), self.act.tok())
        pbuf = [self.sb("p", [128, 512], F, sc) for _ in range(NP)]
        tbuf = [self.sb("pt", [128, 512], F, sc) for _ in range(NT)]
        st = self.sb("st", [128, NSM, 4], F, sc)
        pfree, tfree = [None] * NP, [None] * NT

        def scores(i, u):
            b, bank, free = self.ps.take()
            nk = u["nk"]
            masks = u["masks"]
            t = self.mma(bank[:, 0:nk], u["q"], u["k"], True, not masks, free, *u["toks"], inc=not masks)
            for m, (rhs, c0, n) in enumerate(masks):
                last = m == len(masks) - 1
                t = self.mma(bank[:, c0:c0 + n], self.ident, rhs, False, last, inc=last)
            nm = st[:, i % NSM, 0:1]
            t = self.V(lambda e: e.tensor_reduce(nm, bank[:, 0:nk], AX.X, ALU.max, negate=True), t)
            if u.get("sink") is not None:
                t = self.tt(nm, nm, u["sink"], ALU.min)
            u["b"], u["bank"], u["t"] = b, bank, t

        def exps(i, u):
            nk, p = u["nk"], pbuf[i % NP]
            nm, sm, rc, es = (st[:, i % NSM, c:c + 1] for c in range(4))
            t = self.func(p[:, 0:nk], u["bank"][:, 0:nk], ACT.Exp, u["t"], pfree[i % NP], bias=nm, accum=sm)
            self.ps.give(u["b"], t)
            u["t"] = t

        def norm(i, u):
            t = u["t"]
            nm, sm, rc, es = (st[:, i % NSM, c:c + 1] for c in range(4))
            if u.get("sink") is not None:
                t = self.func(es, u["sink"], ACT.Exp, bias=nm, scale=-1.0)
                self.tt(sm, sm, es, ALU.add, t)
            if u.get("guard"):
                self.ts(sm, sm, 1e-30, None, ALU.max, None, t)
            self.recip(rc, sm, t)
            p = pbuf[i % NP][:, 0:u["nk"]]
            if u["scale"] is None:
                u["t"] = self.ts(p, p, rc, None, ALU.mult, None)
            else:
                u["t"] = self.ts(p, p, rc, u["scale"], ALU.mult, ALU.mult)

        def turn(i, u):
            p, nk = pbuf[i % NP], u["nk"]
            b, bank, free = self.ps.take()
            nb = -(-nk // 128)
            for j in range(nb):
                w = min(128, nk - 128 * j)
                t = self.tr(bank[0:w, 128 * j:128 * j + 128], p[:, 128 * j:128 * j + w], self.ident,
                            u["t"], free, inc=(j == nb - 1))
            pfree[i % NP] = t
            w = min(128, nk)
            dst = tbuf[i % NT][0:w, 0:128 * nb]
            if i % 2:
                t = self.func(dst, bank[0:w, 0:128 * nb], ACT.Copy, t, tfree[i % NT])
            else:
                t = self.V(lambda e: e.tensor_copy(dst, bank[0:w, 0:128 * nb]), t, tfree[i % NT])
            self.ps.give(b, t)
            u["t"] = t

        def values(i, u):
            o, first, last, after = u["out"]()
            n = len(u["v"])
            for j, (v, w) in enumerate(u["v"]):
                t = self.mma(o, v, tbuf[i % NT][0:w, 128 * j:128 * j + 128], first and j == 0, last and j == n - 1,
                             u["t"], inc=(j == n - 1))
            tfree[i % NT] = t
            if after:
                after(t)

        stages = [scores, exps, norm, turn, values]
        for s in range(len(units) + 4):
            self.spend(2)
            for lag in (2, 1, 0, 3, 4):
                i = s - lag
                if 0 <= i < len(units):
                    stages[lag](i, units[i])

    def out_banks(self, heads, evac):
        held = {}

        def out(h, qt, parts, part, nq=4):
            def f():
                pr, par = h // 2, h % 2
                if pr not in held:
                    b, bank, free = self.ps.take()
                    self.pe.wait(free)
                    held[pr] = (b, bank)
                b, bank = held[pr]
                end = par == 1 and qt == nq - 1 and part == parts - 1

                def after(t):
                    evac(pr, b, bank, t)
                return (bank[64 * par:64 * par + 64, 128 * qt:128 * qt + 128], part == 0, part == parts - 1,
                        after if end else None)
            return f
        return out

    def mem_kv(self):
        with ExitStack() as sc:
            mem = self.sb("mem", [128, 8, 256], F, sc)
            mkt = [self.sb("mkt", [128, 2, 256], F, sc) for _ in range(2)]
            t = self.actdma(mem[:, :, :], self.A["memT"].rearrange("(k p) t -> p k t", p=128))
            t = self.rms(lambda k: self.p("mem_norm_g", k), x=lambda k: mem[:, k, :], n=256, t_src=[t] * 8)
            tl = t
            for l in range(2):
                def evac(m, b, bank, t, l=l):
                    self.func(mkt[l][:, m, :], bank[:, 0:256], ACT.Copy, t)
                    t = self.func(self.mv[l][:, m, :], bank[:, 256:512], ACT.Copy)
                    self.ps.give(b, t)
                    self.spend(5)
                self.lin_tok(self.A["w_mem_kv"][l], 0, 8, 0, 512, self.xact_t, 2, evac, tl)
            for l in range(2):
                self.headnorm(lambda t, l=l: mkt[l][:, t, :], 2, 4, lambda pr: self.p("mem_k_norm_g", l),
                              lambda pr: self.mk[l][:, pr, :], self.act.tok())
            self.barrier()

    def mem_units(self, l, qm, out, h0=0):
        return [dict(q=qm[64 * (h % 2):64 * (h % 2) + 64, h // 2, 128 * qt:128 * qt + 128],
                     k=self.mk[l][64 * (h % 2):64 * (h % 2) + 64, h // 2, :], nk=256, masks=[], toks=(),
                     scale=None, v=[(self.mv[l][:, j, 64 * h:64 * h + 64], 128) for j in range(2)],
                     out=out(h0 + h, qt, 1, 0))
                for h in range(4) for qt in range(4)]

    def conformer(self):
        A = self.A
        t_act = self.rms(lambda k: self.p("norm_mix_g0", k))
        W = A["a_w_in"][0]
        with ExitStack() as sc:
            vp = self.sb("vp", [128, 6, 542], F, sc)
            cv = self.sb("cv", [128, 6, 512], F, sc)
            dg = [self.sb("dg", [128, 128], F, sc) for _ in range(4)]
            NV = 5
            tvp, tconv = [None] * 6, [None] * 6

            def tap(j, k):
                src = vp[:, j, k:k + 512]
                if k == 0:
                    t = self.ts(cv[:, j, :], src, self.p("a_dw", 31 * j), self.p("a_dw_b", j), ALU.mult, ALU.add)
                else:
                    t = self.stt(cv[:, j, :], src, self.p("a_dw", 31 * j + k), cv[:, j, :], ALU.mult, ALU.add)
                tconv[j] = t

            def conv_pe(j):
                b, bank = self.bank()
                free = [self.pe.tok()] * 4
                for k in range(31):
                    d = dg[k % 4]
                    t = self.func(d[:, :], self.ident, ACT.Copy, free[k % 4], scale=self.p("a_dw", 31 * j + k))
                    t = free[k % 4] = self.mm(bank[:, :], d[:, :], vp[:, j, k:k + 512], k == 0, k == 30, t, tvp[j],
                                              inc=True)
                tconv[j] = self.func(cv[:, j, :], bank[:, :], ACT.Identity, t, bias=self.p("a_dw_b", j))
                self.ps.give(b, tconv[j])
            qt = self.sb("qt", [128, 4, 256], F, sc)
            qm = self.sb("qm", [128, 2, 512], F, sc)
            sg = [self.sb("sg", [128, 512], F, sc) for _ in range(2)]
            self.V(lambda e: e.memset(vp[:, :, 0:30], 0.0))
            ts = {}
            for p0 in (0, 2, 4):
                def gate(n, b, bank, t, p0=p0):
                    ts[n] = self.func(sg[n][:, :], bank[:, :], ACT.Sigmoid, t, self.dve.tok(),
                                      bias=self.p("a_b_glu", 6 + p0 + n))
                    self.ps.give(b, ts[n])
                    self.spend(5)

                def value(n, b, bank, t, p0=p0):
                    t = self.stt(vp[:, p0 + n, 30:542], bank[:, :], self.p("a_b_glu", p0 + n), sg[n][:, :],
                                 ALU.add, ALU.mult, t, ts[n])
                    self.ps.give(b, t)
                    tvp[p0 + n] = t
                    if p0 + n < NV:
                        self.behind.append(map(lambda k: tap(p0 + n, k), range(31)))
                    self.spend(5)
                self.lin(W, 0, 8, [768 + 128 * (p0 + n) for n in range(2)], self.xact, gate, t_act)
                self.lin(W, 0, 8, [128 * (p0 + n) for n in range(2)], self.xact, value, t_act)

            def evac(m, b, bank, t):
                t = self.func(qt[:, m, :], bank[:, 0:256], ACT.Copy, t)
                self.ps.give(b, t)
            self.lin_tok(W, 0, 8, 1536, 256, self.xact_t, 4, evac, t_act)
            self.spend(10)
            conv_pe(5)
            self.spend(10)
            self.mem_kv()
            self.spend(10)
            self.headnorm(lambda t: qt[:, t, :], 4, 4, lambda pr: self.p("mem_q_norm_g0"),
                          lambda pr: qm[:, pr, :], self.act.tok())
            self.scaled(qm[:, :, :], 0.125)
            def ev(pr, b, bank, t):
                self.ps.give(b, self.split(self.ah[:, 6 + pr, :], self.al[:, 6 + pr, :], bank[:, :], t))
            out = self.out_banks(4, ev)
            self.softmax_units(self.mem_units(0, qm, out), sc)
            self.spend(-1)
            t_mem = self.dve.tok()
            tn = self.layernorm(cv, 6, "eps5", tconv)
            t = self.split_all(6, 512, lambda s, j, *w: self.func(s, cv[:, j, :], ACT.Silu, tn[j], *w,
                                                                  scale=self.p("a_ln_g", j),
                                                                  bias=self.p("a_ln_b", j)))
            self.residual(A["w_out"][0], 8, self.xact, 1.0, t + [t_mem] * 2)
            self.barrier()

    def scaled(self, ap, c):
        return self.ts(ap, ap, c, None, ALU.mult, None, self.act.tok())

    def layernorm(self, v, kt, eps, t_src=None, src=None, finish=True):
        src = v if src is None else src
        if src is self.x:
            t_src = self.xt
        b, bank, t = self.sums(lambda k: src[:, k, :], kt, 512, t_src=t_src, square=False)
        mean = self.rb[:, :]
        tm = self.func(mean, bank[:, :], ACT.Copy, t, self.dve.tok(), scale=-1.0 / (128 * kt))
        self.ps.give(b, tm)
        ts = [self.tt(v[:, k, :], src[:, k, :], mean, ALU.add, tm, self.pe.tok()) for k in range(kt)]
        b, bank, t = self.sums(lambda k: v[:, k, :], kt, 512, t_src=ts)
        self.rstd(mean, bank, b, t, 512, 128.0 * kt, eps)
        return finish and [self.tt(v[:, k, :], v[:, k, :], mean, ALU.mult) for k in range(kt)]

    def relu_mlp(self, l):
        def add(n, bank, t):
            return self.tt(self.x[:, n, :], self.x[:, n, :], bank[:, :], ALU.add, t)
        t = self.rms(lambda k: self.p(f"norm_mlp_g{l}", k))
        self.mlp(None, (self.A["w_mlp_in"][l], 0), self.A["w_mlp_out"][l], 4096, add, t)

    def nsa(self):
        A = self.A
        with ExitStack() as s1:
            kvt = self.sb("kvt", [128, 4, 768], F, s1)
            ksT = self.sb("ksT", [128, 2, 512], F, s1)
            kwT = self.sb("kwT", [128, 2, 512], F, s1)
            kcT = self.sb("kcT", [128, 2, 31], F, s1)
            vcm = self.sb("vcm", [128, 128], F, s1)
            t_act = self.rms(lambda k: self.p("kv_norm_g", k))
            for c0, n in ((0, 512), (512, 256)):
                def evac(m, b, bank, t, c0=c0, n=n):
                    self.ps.give(b, self.func(kvt[:, m, c0:c0 + n], bank[:, 0:n], ACT.Copy, t))
                self.lin_tok(A["w_kv"], 0, 8, c0, n, self.xact_t, 4, evac, t_act)
            self.barrier()
            self.keys(kvt, 256, "k_norm_g1", ksT)
            self.keys(kvt, 512, "k_norm_g2", kwT)
            self.compress(kvt, 0, "pe_k", A["cmp_w1_k"], A["cmp_w2_k"], kcT, vcm, True)
            self.compress(kvt, 128, "pe_v", A["cmp_w1_v"], A["cmp_w2_v"], kcT, vcm, False)
            qT = self.sb("qT", [128, 6, 512], F, s1)
            qm = self.sb("qm", [128, 2, 512], F, s1)
            gts = self.sb("gts", [128, 4, 36], F, s1)
            with ExitStack() as s2:
                qt = self.sb("qt", [128, 4, 1024], F, s2)
                gf = self.sb("gf", [128, 512], F, s2)
                t_act = self.rms(lambda k: self.p("norm_mix_g1", k), again=True)
                W = A["b_w_in"][0]
                for c0 in (0, 512):
                    def evac(m, b, bank, t, c0=c0):
                        self.ps.give(b, self.func(qt[:, m, c0:c0 + 512], bank[:, :], ACT.Copy, t))
                    self.lin_tok(W, 0, 8, c0, 512, self.xact_t, 4, evac, t_act)

                def gate(n, b, bank, t):
                    self.ps.give(b, self.func(gf[:, :], bank[:, :], ACT.Sigmoid, t, bias=self.p("b_gate_b")))
                self.lin(W, 0, 8, [1060 - 128], self.xact, gate, t_act)
                b, bank, free = self.ps.take()
                for t in range(4):
                    tk = self.tr(bank[:, 128 * t:128 * t + 128], gf[:, 128 * t:128 * t + 128], self.ident, free,
                                 self.act.tok(), inc=True)
                src = bank[:, :].rearrange("p (t c) -> p t c", t=4)[:, :, 92:128]
                self.ps.give(b, self.func(gts[:, :, :], src, ACT.Copy, tk))
                self.headnorm(lambda t: qt[:, t, 0:768], 4, 12, lambda pr: self.p("b_q_norm_g"),
                              lambda pr: qT[:, pr, :], self.act.tok())
                self.headnorm(lambda t: qt[:, t, 768:1024], 4, 4, lambda pr: self.p("mem_q_norm_g1"),
                              lambda pr: qm[:, pr, :], self.act.tok())
                self.scaled(qT[:, :, :], 0.125)
                self.scaled(qm[:, :, :], 0.125)
                self.barrier()

            def ev(pr, b, bank, t):
                self.ps.give(b, self.split(self.ah[:, pr, :], self.al[:, pr, :], bank[:, :], t))
            out = self.out_banks(16, ev)
            gv = self.sb("gv", [128, 36], F, s1)
            self.ts(gv[:, :], gts[:, 0, :], self.c("rowok"), None, ALU.mult, None, self.act.tok())
            units = []
            for h in range(12):
                g, par = h // 6, h % 2
                s = slice(64 * par, 64 * par + 64)
                for qi in range(4):
                    nk = 128 * (qi + 1)
                    q = qT[s, h // 2, 128 * qi:128 * qi + 128]
                    cm = self.c("cmpmask")[:, 31 * qi:31 * qi + 31]
                    gc = gv if qi == 0 else gts[:, qi, :]
                    units.append(dict(q=q, k=kcT[s, g, :], nk=31, masks=[(cm, 0, 31)], toks=(), guard=True,
                                      scale=gc[:, 3 * h:3 * h + 1], v=[(vcm[0:31, 64 * g:64 * g + 64], 31)],
                                      out=out(h, qi, 3, 0)))
                    for part, (kT, vc, gi) in enumerate(((ksT, 384, 1), (kwT, 640, 2))):
                        units.append(dict(
                            q=q, k=kT[s, g, 0:nk], nk=nk, masks=[(self.c("causal"), 128 * qi, 128)], toks=(),
                            guard=True, scale=gts[:, qi, 3 * h + gi:3 * h + gi + 1],
                            v=[(kvt[:, j, vc + 64 * g:vc + 64 * g + 64], 128) for j in range(qi + 1)],
                            out=out(h, qi, 3, 1 + part)))
            units += self.mem_units(1, qm, out, 12)
            self.softmax_units(units, s1)
            self.barrier()
            self.residual(A["w_out"][1], 8, self.xact, 1.0)
            self.barrier()

    def keys(self, kvt, c0, gain, dst, *toks):
        with ExitStack() as sc:
            kd = self.sb("kd", [128, 4, 2, 2, 64], F, sc)
            for t in range(4):
                src = kvt[:, t, c0:c0 + 128].rearrange("p (g d) -> p g d", g=2)
                for u in range(2):
                    self.V(lambda e, o=kd[:, t, :, u, :], s=src: e.tensor_copy(o, s))
            self.headnorm(lambda t: kd[:, t, :, :, :].rearrange("p g u d -> p (g u d)"), 4, 4,
                          lambda pr: self.p(gain), lambda pr: dst[:, pr, :], self.dve.tok())

    def compress(self, kvt, c0, pe, W1, W2, kcT, vcm, is_k):
        with ExitStack() as sc:
            kd = self.sb("kd", [128, 4, 2, 2, 64], F, sc)
            kb = self.sb("kb", [128, 2, 512], F, sc)
            bx = self.sb("bx", [128, 16, 2, 31], F, sc)
            h1 = self.sb("h1", [128, 2, 62], F, sc)
            w2 = self.sb("w2", [128, 2, 64], F, sc)
            tw = self.actdma(w2[:, :, :], W2.rearrange("(k p) n -> p k n", p=128))
            for t in range(4):
                src = kvt[:, t, c0:c0 + 128].rearrange("p (g d) -> p g d", g=2)
                for u in range(2):
                    self.V(lambda e, o=kd[:, t, :, u, :], s=src: e.tensor_copy(o, s))
            for g in range(2):
                b, bank, free = self.ps.take()
                for t in range(4):
                    tk = self.tr(bank[:, 128 * t:128 * t + 128], kd[:, t, g, :, :].rearrange("p u d -> p (u d)"),
                                 self.ident, free, self.dve.tok(), inc=True)
                self.func(kb[0:64, g, :], bank[0:64, :], ACT.Copy, tk)
                t = self.func(kb[64:128, g, 0:511], bank[64:128, 1:512], ACT.Copy)
                self.ps.give(b, t)
            for g in range(2):
                for l in range(16):
                    tb = self.ts(bx[:, l, g, :], kb[:, g, 2 * l:2 * l + 481:16], self.p(pe, l), None, ALU.add, None, t)
            banks = [self.ps.take() for _ in range(2)]
            for k0 in (0, 8):
                i, w, landed = self.slab_raw(W1, 128 * k0, 8, 0, 256)
                for m in range(2):
                    for k in range(8):
                        tk = self.mm(banks[m][1][:, 0:62], w[:, k, 128 * m:128 * m + 128],
                                     bx[:, k0 + k, :, :].rearrange("p g n -> p (g n)"), k0 + k == 0, k0 + k == 15,
                                     landed, banks[m][2], tb, inc=(k == 7))
                self.raw_ring.done(i, self.pe.tok())
            for m in range(2):
                t = self.func(h1[:, m, :], banks[m][1][:, 0:62], ACT.Gelu_apprx_tanh, self.pe.tok())
                self.ps.give(banks[m][0], t)
            b, bank, free = self.ps.take()
            for g in range(2):
                for k in range(2):
                    tk = self.mma(bank[0:31, 64 * g:64 * g + 64], h1[:, k, 31 * g:31 * g + 31], w2[:, k, :],
                                  k == 0, k == 1, free, t, tw, inc=True)
            if not is_k:
                self.ps.give(b, self.func(vcm[0:31, :], bank[0:31, 0:128], ACT.Copy, tk))
            else:
                kc = self.sb("kc", [128, 2, 2, 64], F, sc)
                sq = self.sb("sq", [128, 128], F, sc)
                t1 = self.func(sq[0:31, :], bank[0:31, 0:128], ACT.Square, tk)
                ss = self.sm[0:31, 0:2]
                i3 = sq[0:31, :].rearrange("p (g d) -> p g d", g=2)
                t2 = self.V(lambda e: e.tensor_reduce(ss, i3, AX.X, ALU.add), t1)
                t2 = self.func(ss, ss, ACT.Sqrt, t2, scale=1.0 / 64, bias=self.c("eps6")[0:31, :])
                self.recip(ss, ss, t2)
                for g in range(2):
                    for u in range(2):
                        t2 = self.ts(kc[0:31, g, u, :], bank[0:31, 64 * g:64 * g + 64], self.sm[0:31, g:g + 1], None,
                                     ALU.mult, None)
                self.ps.give(b, t2)
                b, bank2, free = self.ps.take()
                for g in range(2):
                    tk = self.tr(bank2[:, 32 * g:32 * g + 31], kc[0:31, g, :, :].rearrange("p u d -> p (u d)"),
                                 self.ident[0:31, 0:31], free, t2, inc=True)
                src = bank2[:, 0:64].rearrange("p (g n) -> p g n", g=2)[:, :, 0:31]
                self.ps.give(b, self.func(kcT[:, :, :], src, ACT.Copy, tk, scale=self.p("k_norm_g0")))
            self.barrier()

    def block1(self):
        with ExitStack() as s0:
            self.acts(s0)
            self.mk = [self.sb("mk", [128, 2, 256], F, s0) for _ in range(2)]
            self.mv = [self.sb("mv", [128, 2, 256], F, s0) for _ in range(2)]
            self.conformer()
            self.relu_mlp(0)
            self.nsa()
            self.relu_mlp(1)
    def swiglu2(self, which):
        A = self.A
        with ExitStack() as s0:
            self.acts(s0)

            def add(n, bank, t):
                return self.stt(self.x[:, n, :], bank[:, :], 0.5, self.x[:, n, :], ALU.mult, ALU.add, t)
            t = self.rms(lambda k: self.p(f"{which}_norm", k))
            self.mlp((A[f"{which}_w_gate_2"][0], 0), (A[f"{which}_w_up_2"][0], 0), A[f"{which}_w_down_2"][0], 2816,
                     add, t)

    def slot_dma(self, i, dst, src, *toks):
        self.act.dma(lambda e: e.dma_start(dst, src), self.s_scr[i], *toks)
        self.n_scr[i] += 16
        return (self.s_scr[i], self.n_scr[i])

    def mixer2(self):
        A = self.A
        W = A["w_in_2"][0]
        gates = self.nc.dram_tensor("gates_2", (16, 128, 512), F).ap()
        saved = {}
        with ExitStack() as s0:
            yA = self.sb("yA", [128, 4, 512], F, s0)
            yR = self.sb("yR", [128, 4, 512], F, s0)
            with ExitStack() as s1:
                r = self.sb("r", [128, 4, 512], F, s1)
                k = self.sb("k", [128, 4, 512], F, s1)
                v = self.sb("v", [128, 4, 576], F, s1)
                sA = self.sb("sA", [128, 2, 512], F, s1)
                with ExitStack() as s2:
                    at = self.sb("at", [128, 4, 768], F, s2)
                    with ExitStack() as s3:
                        self.acts(s3)
                        pb = [self.sb("pb", [128, 513], F, s3) for _ in range(2)]
                        t_act = self.rms(lambda k: self.p("mix_norm", k))

                        def gate(n, b, bank, t):
                            i, rd = self.scr_ring.next()
                            t = self.func(self.scr[i][:, :], bank[:, :], ACT.Sigmoid, t, *rd)
                            self.ps.give(b, t)
                            saved[n] = self.slot_dma(i, gates[n], self.scr[i][:, :], t)
                            self.scr_ring.done(i, saved[n])
                        self.lin(W, 0, 8, [2464 + 128 * n for n in range(16)], self.xact, gate, t_act)
                        for c0, n in ((0, 512), (512, 256)):
                            def evac(m, b, bank, t, c0=c0, n=n):
                                self.ps.give(b, self.func(at[:, m, c0:c0 + n], bank[:, 0:n], ACT.Copy, t))
                            self.lin_tok(W, 0, 8, 1696 + c0, n, self.xact_t, 4, evac, t_act)
                        for i in range(2):
                            self.V(lambda e, i=i: e.memset(pb[i][:, 0:1], 0.0))
                        tm = self.V(lambda e: e.memset(v[:, :, 0:64], 0.0))
                        rd = [tm, tm]

                        def shifted(n, b, bank, t):
                            q = pb[n % 2]
                            t = self.func(q[:, 1:513], bank[:, :], ACT.Copy, t, rd[n % 2])
                            self.ps.give(b, t)
                            i, r2 = self.scr_ring.next()
                            s = self.scr[i][:, :]
                            self.tt(s, q[:, 0:512], q[:, 1:513], ALU.subtract, t, *r2)
                            dst = [r[:, n % 4, :], k[:, n % 4, :], v[:, n % 4, 64:576], sA[:, n % 4 % 2, :]][n // 4]
                            rd[n % 2] = self.stt(dst, s, self.p("mu", n), q[:, 1:513], ALU.mult, ALU.add)
                            self.scr_ring.done(i, rd[n % 2])
                        self.lin(W, 0, 8, [128 * n for n in range(14)], self.xact, shifted, t_act)
                        self.barrier()
                    self.swa(at, yA)
                self.rwkv(r, k, v, sA, yR)
            with ExitStack() as s1:
                yh, yl = self.sb("yh", [128, 8, 512], R, s1), self.sb("yl", [128, 8, 512], R, s1)
                self.acts(s1)
                gr = self.sb("gr", [128, 4, 512], F, s1)
                merged = []
                for j in range(4):
                    self.split(yh[:, j, :], yl[:, j, :], yR[:, j, :])
                for j in range(4):
                    ty = self.split(yh[:, 4 + j, :], yl[:, 4 + j, :], yA[:, j, :])
                for half in range(2):
                    c = [512 * half + 128 * n for n in range(4)]
                    for br, name in enumerate(("w_branch_rwkv_2", "w_branch_attn_2")):
                        def evac(n, b, bank, t, half=half, br=br):
                            i, rd = self.scr_ring.next()
                            s = self.scr[i][:, :]
                            g = 8 * br + 4 * half + n
                            tg = self.slot_dma(i, s, gates[g], saved[g], *rd)
                            if br == 0:
                                t = self.tt(gr[:, n, :], bank[:, :], s, ALU.mult, t, tg)
                                self.ps.give(b, t)
                            else:
                                t = self.tt(s, bank[:, :], s, ALU.mult, t, tg)
                                self.ps.give(b, t)
                                t = self.tt(s, s, gr[:, n, :], ALU.add)
                                t = self.split(self.ah[:, 4 * half + n, :], self.al[:, 4 * half + n, :], s, t)
                                merged.append(t)
                            self.scr_ring.done(i, t)
                        self.lin(A[name][0], 0, 4, c, lambda k, br=br: (yh[:, 4 * br + k, :], yl[:, 4 * br + k, :]),
                                 evac, ty)
                self.residual(A["w_out_2"][0], 8, self.xact, 1.0, merged)
                self.barrier()

    def swa(self, at, yA):
        with ExitStack() as sc:
            qT = self.sb("qT", [128, 4, 512], F, sc)
            kT = self.sb("kT", [128, 2, 512], F, sc)
            ns = self.sb("ns", [128, 8], F, sc)
            self.headnorm(lambda t: at[:, t, 0:512], 4, 8, lambda pr: self.p("attn_q_norm"),
                          lambda pr: qT[:, pr, :])
            self.keys(at, 512, "attn_k_norm", kT)
            self.scaled(qT[:, :, :], 0.125)
            self.ts(ns[:, :], self.p("sinks", 0, 8), -1.0, None, ALU.mult, None)

            def ev(pr, b, bank, t):
                self.ps.give(b, self.func(yA[:, pr, :], bank[:, :], ACT.Copy, t))
            out = self.out_banks(8, ev)
            units = []
            for h in range(8):
                g, s = h // 4, slice(64 * (h % 2), 64 * (h % 2) + 64)
                for qi in range(4):
                    j0 = max(qi - 1, 0)
                    nk = 128 * (qi + 1 - j0)
                    masks = [(self.c("causal"), nk - 128, 128)] + ([(self.c("swaprev"), 0, 128)] if qi else [])
                    units.append(dict(
                        q=qT[s, h // 2, 128 * qi:128 * qi + 128], k=kT[s, g, 128 * j0:128 * (qi + 1)], nk=nk,
                        masks=masks, toks=(), scale=None, sink=ns[:, h:h + 1],
                        v=[(at[:, j, 640 + 64 * g:704 + 64 * g], 128) for j in range(j0, qi + 1)],
                        out=out(h, qi, 1, 0)))
            self.softmax_units(units, sc)
            self.barrier()

    def rwkv(self, r, k, v, sA, yR):
        A = self.A
        with ExitStack() as sc:
            rwc = self.sb("rwc", [128, NRWC], F, sc)
            cc = lambda n: rwc[:, RWC[n][0]:RWC[n][0] + RWC[n][1]]
            wl = self.sb("wl", [128, 2, 512], F, sc)
            self.actdma(rwc[:, :], A["rwc"])
            self.actdma(wl[0:32, 0, :], A["rwkv_w_lora_up_2"][0])
            self.actdma(wl[32:64, 0, :], A["rwkv_a_lora_up_2"][0])
            self.actdma(wl[64:128, 0, :], A["rwkv_g_lora_up_2"][0][0:64, :])
            tw = self.actdma(wl[0:32, 1, :], A["rwkv_g_lora_up_2"][0][64:96, :])
            for q in (self.pe, self.dve):
                q.wait(tw)
            self.func(sA[0:32, 0, :], sA[0:32, 0, :], ACT.Tanh)
            self.func(sA[64:128, 0, :], sA[64:128, 0, :], ACT.Sigmoid)
            self.func(sA[0:32, 1, :], sA[0:32, 1, :], ACT.Sigmoid)
            keep = self.sb("keep", [128, 512], F, sc)
            self.V(lambda e: e.memset(keep[:, :], 1.0))
            self.V(lambda e: e.memset(keep[:, 0:512:64], 0.0))
            shapes = dict(c=[512], a=[512], g=[512], kk=[512], kp=[512], bon=[512], Pi=[512], Xs=[64], ST=[2, 64],
                          SP=[64], AR=[8, 128], BK=[8, 128], BT=[8, 128], UV=[8, 128], M=[16, 128], D=[8, 128],
                          Pp=[8, 65])
            B = [{n: self.sb(n, [128, *s], F, sc) for n, s in shapes.items()}, {}]
            B[1] = self.borrow(shapes)
            self.pe.wait(self.act.tok(), self.dve.tok())
            ends = [(), ()]

            def pairs(slot):
                for j in range(slot, 4, 2):
                    for q in (self.pe, self.act, self.dve):
                        q.wait(*ends[slot])
                    yield from self.rwkv_tile(j, slot, r[:, j, :], k[:, j, :], v[:, j, :], sA, wl, cc, keep,
                                              B[slot], yR[:, j, :])
                    ends[slot] = tuple(q.tok() for q in (self.pe, self.act, self.dve))
            for _ in self.rounds([pairs(0), pairs(1)]):
                pass
            self.give_back(*ends[0], *ends[1])
            self.barrier()

    @staticmethod
    def rounds(gens):
        while gens:
            gens = [g for g in gens if next(g, 0) is None]
            yield

    def bank(self):
        b, bank, free = self.ps.take()
        self.pe.wait(free)
        return b, bank

    def rwkv_tile(self, j, slot, r, k, v, sA, wl, cc, keep, B, y):
        js = slice(128 * j, 128 * j + 128)
        c, a, g, kk, kp, bon, Pi = (B[n][:, :] for n in ("c", "a", "g", "kk", "kp", "bon", "Pi"))
        Pp, AR, BK, BT, UV, M, Xs, ST, SP, D = (B[n] for n in ("Pp", "AR", "BK", "BT", "UV", "M", "Xs", "ST", "SP", "D"))
        v0 = v[:, 64:576]
        ch = lambda ap: ap.rearrange("p (c t) -> p c t", t=64)
        b, bank = self.bank()
        t = self.mm(bank[:, :], wl[0:32, 0, js], sA[0:32, 0, :], True, True, inc=True)
        yield
        t = self.func(c, bank[:, :], ACT.Sigmoid, t, bias=self.p("rwkv_w0", j))
        self.ps.give(b, t)
        self.ts(c, c, -0.6065306597126334, None, ALU.mult, None, t)
        tc = self.V(lambda e: e.tensor_tensor_scan(Pi, keep[:, :], c, 0.0, ALU.mult, ALU.add))
        b, bank = self.bank()
        t = self.mm(bank[:, :], wl[32:64, 0, js], sA[32:64, 0, :], True, True, inc=True)
        yield
        ta = self.func(a, bank[:, :], ACT.Sigmoid, t, bias=self.p("rwkv_a0", j))
        self.ps.give(b, ta)
        b, bank = self.bank()
        self.mm(bank[:, :], wl[64:128, 0, js], sA[64:128, 0, :], True, False)
        t = self.mm(bank[:, :], wl[0:32, 1, js], sA[0:32, 1, :], False, True, inc=True)
        yield
        self.ps.give(b, self.func(g, bank[:, :], ACT.Copy, t))
        self.V(lambda e: e.memset(Pp[:, :, 0:1], 1.0))
        self.func(Pp[:, :, 1:65], ch(Pi), ACT.Exp, tc)
        tp = self.func(Pi, Pi, ACT.Exp, scale=-1.0)
        t = self.ts(kk, k, self.p("rwkv_k_k", j), None, ALU.mult, None)
        t = self.func(c, kk, ACT.Square, t)
        b, bank = self.bank()
        t = self.mm(bank[:, :], self.bones, c, True, True, t, inc=True)
        yield
        t = self.func(c, bank[:, :], ACT.Sqrt, t)
        self.ps.give(b, t)
        self.ts(c, c, 1e-12, None, ALU.max, None, t)
        self.recip(c, c)
        self.tt(kk, kk, c, ALU.mult)
        self.ts(kp, a, -1.0, self.p("rwkv_k_a", j), ALU.add, ALU.mult, ta)
        self.stt(kp, kp, 1.0, k, ALU.add, ALU.mult)
        self.tt(a, kk, a, ALU.mult)
        t = self.stt(c, r, self.p("rwkv_r_k", j), kp, ALU.mult, ALU.mult)
        b, bank = self.bank()
        t = self.mm(bank[:, :], self.bones, c, True, True, t, inc=True)
        yield
        self.ps.give(b, self.tt(bon, bank[:, :], v0, ALU.mult, t))
        self.stt(AR[:, :, 0:64], ch(kk), -1.0, Pp[:, :, 0:64], ALU.mult, ALU.mult, tp)
        self.tt(AR[:, :, 64:128], ch(r), Pp[:, :, 1:65], ALU.mult)
        self.tt(BK[:, :, 0:64], ch(a), ch(Pi), ALU.mult)
        tb = self.tt(BK[:, :, 64:128], ch(kp), ch(Pi), ALU.mult)
        self.pe.wait(tb)
        for q in range(2):
            b, bank = self.bank()
            for i in range(4):
                cx = 4 * q + i
                t = self.tr(bank[:, 128 * i:128 * i + 128], v[:, 64 * cx:64 * cx + 128], self.ident, inc=True)
            yield
            self.ps.give(b, self.func(UV[64:128, 4 * q:4 * q + 4, :],
                                      bank[64:128, :].rearrange("p (c n) -> p c n", c=4), ACT.Copy, t))
            b, bank = self.bank()
            for i in range(4):
                t = self.tr(bank[:, 128 * i:128 * i + 128], BK[:, 4 * q + i, :], self.ident, inc=True)
            yield
            self.ps.give(b, self.func(BT[:, 4 * q:4 * q + 4, :], bank[:, :].rearrange("p (c n) -> p c n", c=4),
                                      ACT.Copy, t))
        self.V(lambda e: e.memset(UV[0:64, :, :], 0.0))
        for q in range(4):
            b, bank = self.bank()
            hh = q // 2
            hs = slice(64 * hh, 64 * hh + 64)
            for i in range(4):
                cx = 4 * (q % 2) + i
                t = self.mma(bank[:, 128 * i:128 * i + 128], BK[hs, cx, :], AR[hs, cx, :], True, True, inc=(i == 3))
            yield
            t = self.tt(M[:, 4 * q:4 * q + 4, :], bank[:, :].rearrange("p (i n) -> p i n", i=4),
                        cc("gram").unsqueeze(1).to_broadcast([128, 4, 128]), ALU.mult, t)
            self.ps.give(b, t)
        yield from self.rounds([
            self.inverse(0, BK, AR, D, cc, [Pi, kk, c, a]),
            self.inverse(1, BK, AR, D, cc, [kp, r, k, y])])
        ty, tS = None, self.V(lambda e: e.memset(ST[:, 0, :], 0.0))
        yb = [self.bank() for _ in range(2)]
        self.pe.wait(self.dve.tok(), self.act.tok())
        for cx in range(8):
            so, sn = ST[:, cx % 2, :], ST[:, (cx + 1) % 2, :]
            b, bank = self.bank()
            for hh in range(2):
                hs = slice(64 * hh, 64 * hh + 64)
                self.mma(bank[hs, 0:64], M[:, 8 * hh + cx, 0:64], UV[:, cx, hs], True, False)
            for hh in range(2):
                hs = slice(64 * hh, 64 * hh + 64)
                t = self.mma(bank[hs, 0:64], AR[hs, cx, 0:64], so[hs, :], False, True, tS, inc=(hh == 1))
            yield
            t = self.V(lambda e, bank=bank: e.tensor_copy(Xs[:, :], bank[:, 0:64]), t)
            self.ps.give(b, t)
            pc = Pp[:, cx, 64:65]
            self.ts(SP[:, :], so, pc, None, ALU.mult, None)
            b, bank = self.bank()
            for hh in range(2):
                hs = slice(64 * hh, 64 * hh + 64)
                t = self.mma(bank[0:64, hs], D[:, cx, hs], Xs[:, :], True, True, t, inc=(hh == 1))
            yield
            tu = self.V(lambda e, bank=bank, cx=cx: e.tensor_copy(UV[0:64, cx, :], bank[0:64, 0:128]), t)
            self.ps.give(b, tu)
            b, bank = self.bank()
            for hh in range(2):
                hs = slice(64 * hh, 64 * hh + 64)
                t = self.mma(bank[hs, 0:64], BT[:, cx, hs], UV[:, cx, hs], True, True, tu, inc=(hh == 1))
            yield
            tS = self.stt(sn, bank[:, 0:64], pc, SP[:, :], ALU.mult, ALU.add, t, ty)
            self.ps.give(b, tS)
            ps = slice(64 * (cx % 2), 64 * (cx % 2) + 64)
            for hh in range(2):
                hs = slice(64 * hh, 64 * hh + 64)
                o = yb[hh][1][ps, 64 * (cx // 2):64 * (cx // 2) + 64]
                self.mma(o, AR[hs, cx, 64:128], so[hs, :], True, False)
                ty = self.mma(o, M[:, 8 * hh + cx, 64:128], UV[:, cx, hs], False, True, inc=(hh == 1))
        ys = B["kk"]
        y3 = ys[:, :].rearrange("p (h d) -> p h d", d=64)
        y4 = ys[:, :].rearrange("p (q h d) -> p q h d", h=2, d=64)
        for hh in range(2):
            t = self.func(y4[:, :, hh, :], yb[hh][1][:, 0:256].rearrange("p (q d) -> p q d", d=64), ACT.Copy, ty,
                          tS)
            self.ps.give(yb[hh][0], t)
        mu, sq = self.sm[:, 8 * slot:8 * slot + 8], B["kp"]
        bc = mu.unsqueeze(2).to_broadcast([128, 8, 64])
        self.V(lambda e: e.tensor_reduce(mu, y3, AX.X, ALU.add), t)
        self.ts(mu, mu, -1.0 / 64, None, ALU.mult, None)
        t = self.tt(y3, y3, bc, ALU.add)
        t = self.func(sq[:, :], ys[:, :], ACT.Square, t)
        q3 = sq[:, :].rearrange("p (h d) -> p h d", d=64)
        t = self.V(lambda e: e.tensor_reduce(mu, q3, AX.X, ALU.add), t)
        t = self.func(mu, mu, ACT.Sqrt, t, scale=1.0 / 64, bias=self.c("epsg"))
        self.recip(mu, mu, t)
        t = self.tt(y3, y3, bc, ALU.mult)
        b, bank = self.bank()
        for i in range(4):
            t2 = self.tr(bank[:, 128 * i:128 * i + 128], ys[:, 128 * i:128 * i + 128], self.ident, t, inc=True)
        yield
        t = self.ts(y, bank[:, :], self.p("rwkv_ln_w", j), self.p("rwkv_ln_b", j), ALU.mult, ALU.add, t2)
        self.ps.give(b, t)
        self.tt(y, y, bon, ALU.add)
        self.tt(y, y, g, ALU.mult)

    def inverse(self, q, BK, AR, D, cc, bufs):
        N, DT, ZT, NL = (x.rearrange("p (i n) -> p i n", i=4) for x in bufs)
        four = lambda n: cc(n).unsqueeze(1).to_broadcast([128, 4, 128])
        idb = self.ident.unsqueeze(1).to_broadcast([128, 4, 128])
        self.V(lambda e: e.memset(N[:, :, :], 0.0))
        Dq = D[:, 4 * q:4 * q + 4, :]
        b, bank = self.bank()
        for i in range(4):
            for hh in range(2):
                hs = slice(64 * hh, 64 * hh + 64)
                t = self.mma(bank[hs, 128 * i + 64 * hh:128 * i + 64 * hh + 64], BK[hs, 4 * q + i, 0:64],
                             AR[hs, 4 * q + i, 0:64], True, True, inc=(i == 3))
        yield
        for hh in range(2):
            hs = slice(64 * hh, 64 * hh + 64)
            t = self.tt(N[hs, :, hs], bank[hs, :].rearrange("p (i n) -> p i n", i=4)[:, :, hs],
                        cc("upper")[hs, :].unsqueeze(1).to_broadcast([64, 4, 64]), ALU.mult, t)
        self.ps.give(b, t)
        t = self.tt(NL[:, :, :], N[:, :, :], four("lev0"), ALU.mult)
        self.tt(Dq, NL[:, :, :], idb, ALU.add)
        b, bank = self.bank()
        for i in range(4):
            t2 = self.tr(bank[:, 128 * i:128 * i + 128], NL[:, i, :], self.ident, t, inc=(i == 3))
        yield
        b4 = bank[:, :].rearrange("p (i n) -> p i n", i=4)
        t = self.tt(DT[:, :, :], b4, idb, ALU.add, t2)
        self.ps.give(b, t)
        for l in range(1, 6):
            t = self.tt(NL[:, :, :], N[:, :, :], four(f"lev{l}"), ALU.mult)
            b, bank = self.bank()
            for i in range(4):
                t2 = self.mma(bank[:, 128 * i:128 * i + 128], NL[:, i, :], DT[:, i, :], True, True, t,
                              inc=(i == 3))
            yield
            t = self.func(ZT[:, :, :], bank[:, :].rearrange("p (i n) -> p i n", i=4), ACT.Copy, t2)
            self.ps.give(b, t)
            b, bank = self.bank()
            for i in range(4):
                t1 = self.mma(bank[:, 128 * i:128 * i + 128], ZT[:, i, :], Dq[:, i, :], True, True, t,
                              inc=(i == 3))
            if l < 5:
                b2, bank2 = self.bank()
                for i in range(4):
                    t2 = self.mma(bank2[:, 128 * i:128 * i + 128], Dq[:, i, :], ZT[:, i, :], True, True,
                                  inc=(i == 3))
                yield
            t = self.tt(Dq, Dq, bank[:, :].rearrange("p (i n) -> p i n", i=4), ALU.add, t1, t2)
            self.ps.give(b, t)
            if l < 5:
                t = self.tt(DT[:, :, :], DT[:, :, :], bank2[:, :].rearrange("p (i n) -> p i n", i=4),
                            ALU.add, t2)
                self.ps.give(b2, t)

    def block2(self):
        self.swiglu2("ffn1")
        self.mixer2()
        self.swiglu2("ffn2")
        b, bank, t = self.x_squares()
        self.rstd(self.rb[:, :], bank, b, t, 512, 1024.0, "eps6")
        for k in range(8):
            self.xt[k] = self.stt(self.x[:, k, :], self.x[:, k, :], self.p("final_norm", k), self.rb[:, :], ALU.mult, ALU.mult)
        self.barrier()
    def modulation(self):
        self.mods, self.mc = self.sb("mods", [128, 48]), self.sb("mc", [128, 8])
        macc = self.sb("macc", [128, 512])
        self.func(self.mc[:, :], self.p("c", 0, 8), ACT.Silu)
        free = [None, None]
        tc = self.act.tok()

        def step(n, half):
            acc = macc[:, :]
            i, w, landed = self.slab_raw(self.A["w_ada_3"][0], 512 * half, 4, 512 * n, 512)
            for k in range(4):
                kk = 4 * half + k
                if kk == 0:
                    t = self.ts(acc, w[:, k, :], self.mc[:, 0:1], None, ALU.mult, None, landed, tc, free[0])
                else:
                    t = self.stt(acc, w[:, k, :], self.mc[:, kk:kk + 1], acc, ALU.mult, ALU.add, landed)
            self.raw_ring.done(i, t)
            free[1] = t

        def total(n):
            b, bank, fr = self.ps.take()
            for m in range(4):
                t2 = self.mma(bank[:, m:m + 1], macc[:, 128 * m:128 * m + 128], self.ones[:, 0:1], True, True, fr,
                              free[1], inc=(m == 3))
            free[0] = t2
            self.ps.give(b, self.tt(self.mods[:, 4 * n:4 * n + 4], bank[:, 0:4], self.p("b_ada", 4 * n, 4), ALU.add,
                                    t2))
        for n in range(12):
            self.asides += [lambda n=n: step(n, 0), lambda n=n: step(n, 1), lambda n=n: total(n)]

    def mod(self, i, k):
        return self.mods[:, 8 * i + k:8 * i + k + 1]

    def modulated(self, sc, sh, xn=None):
        with ExitStack() as s0:
            if xn is None:
                xn = self.sb("xn", [128, 8, 512], F, s0)
            self.layernorm(xn, 8, "eps5", src=self.x, finish=False)
            t = self.split_all(
                8, 512, lambda s, k, *w: self.stt(s, xn[:, k, :], self.mod(sc, k), self.rb[:, :], ALU.mult,
                                                  ALU.mult, *w), bias=lambda k: self.mod(sh, k))
        return t

    def scale_x(self, c):
        for k in range(8):
            self.xt[k] = t = self.ts(self.x[:, k, :], self.x[:, k, :], c, None, ALU.mult, None)
        return t

    def post_norm(self, g, b):
        self.layernorm(self.x, 8, "eps5", src=self.x, finish=False)
        for k in range(8):
            x = self.x[:, k, :]
            self.stt(x, x, self.p(g, k), self.rb[:, :], ALU.mult, ALU.mult)
            self.xt[k] = self.ts(x, x, self.p(b, k), None, ALU.add, None)

    def block3(self):
        A = self.A
        alpha = 2.0 ** 0.25
        while self.asides:
            self.aside()
        for i in (1, 2, 4, 5):
            self.ts(self.mods[:, 8 * i:8 * i + 8], self.mods[:, 8 * i:8 * i + 8], 1.0, None, ALU.add, None)
        self.barrier()
        self.mixer3(alpha)
        self.post_norm("ln1_g", "ln1_b")
        with ExitStack() as s0:
            self.acts(s0)
            t = self.modulated(4, 3)
            self.scale_x(alpha)

            def add(n, bank, t):
                return self.stt(self.x[:, n, :], bank[:, :], self.mod(5, n), self.x[:, n, :], ALU.mult, ALU.add, t)
            self.mlp((A["w_ffn_in_3"][0], 0), (A["w_ffn_in_3"][0], 2816), A["w_ffn_out_3"][0], 2816, add, t, False)
        self.post_norm("ln2_g", "ln2_b")

    def mixer3(self, alpha):
        A = self.A
        W = A["w_in_3"][0]
        gates = self.nc.dram_tensor("gates_3", (16, 128, 512), F).ap()
        saved = {}
        with ExitStack() as s0:
            yS = self.sb("yS", [128, 4, 512], F, s0)
            u = self.sb("u", [128, 4, 512], F, s0)
            yM = self.sb("yM", [128, 4, 512], F, s0)
            tables = ExitStack()
            self.ssm_tables(tables)
            self.behind = [self.ssm_setup()]
            with ExitStack() as s1:
                qk = self.sb("qk", [128, 8, 512], F, s1)
                q, k = qk[:, 0:4, :], qk[:, 4:8, :]
                v = self.sb("v", [128, 4, 512], F, s1)
                with ExitStack() as s2:
                    self.acts(s2)
                    t_act = self.modulated(1, 0, qk)

                    def gate(n, b, bank, t):
                        i, rd = self.scr_ring.next()
                        t = self.func(self.scr[i][:, :], bank[:, :], ACT.Sigmoid, t, *rd)
                        self.ps.give(b, t)
                        saved[n] = self.slot_dma(i, gates[n], self.scr[i][:, :], t)
                        self.scr_ring.done(i, saved[n])
                        self.spend(4)
                    self.lin(W, 0, 8, [2048 + 128 * n for n in range(16)], self.xact, gate, t_act)

                    def feat(n, b, bank, t):
                        dst, sc = [(q, 0.125), (k, 1.0), (u, 1.0)][n // 4]
                        self.ps.give(b, self.func(dst[:, n % 4, :], bank[:, :], ACT.Copy, t, scale=sc))
                        self.spend(4)
                    self.lin(W, 0, 8, [128 * n for n in range(8)] + [1536 + 128 * n for n in range(4)], self.xact,
                             feat, t_act)

                    def tok(m, b, bank, t):
                        self.ps.give(b, self.func(v[:, m, :], bank[:, :], ACT.Copy, t))
                    self.lin_tok(W, 0, 8, 1024, 512, self.xact_t, 4, tok, t_act)
                    self.barrier()
                self.stick(q, k, v, yS, s1)
                self.barrier()
            self.spend(-1)
            self.ssm(u, yM)
            tables.close()
            with ExitStack() as s1:
                yh, yl = self.sb("yh", [128, 8, 512], R, s1), self.sb("yl", [128, 8, 512], R, s1)
                for j in range(4):
                    ty = self.split(yh[:, j, :], yl[:, j, :], yM[:, j, :])

                def glu(n, b, bank, t):
                    i, rd = self.scr_ring.next()
                    s = self.scr[i][:, :]
                    t = self.func(s, bank[:, :], ACT.Sigmoid, t, *rd, bias=self.p("b_glu", n))
                    self.ps.give(b, t)
                    t = self.tt(s, s, yM[:, n, :], ALU.mult, t)
                    self.scr_ring.done(i, self.split(yh[:, 4 + n, :], yl[:, 4 + n, :], s, t))
                self.lin(A["w_glu_3"][0], 0, 4, [128 * n for n in range(4)],
                         lambda k: (yh[:, k, :], yl[:, k, :]), glu, ty)
                for j in range(4):
                    ty = self.split(yh[:, j, :], yl[:, j, :], yS[:, j, :], self.pe.tok())
                self.acts(s1)
                gr = self.sb("gr", [128, 4, 512], F, s1)
                merged = []
                for half in range(2):
                    c = [512 * half + 128 * n for n in range(4)]
                    for br, name in enumerate(("w_sb_up_3", "w_ssm_up_3")):
                        def evac(n, b, bank, t, half=half, br=br):
                            i, rd = self.scr_ring.next()
                            s = self.scr[i][:, :]
                            g = 8 * br + 4 * half + n
                            tg = self.slot_dma(i, s, gates[g], saved[g], *rd)
                            if br == 0:
                                t = self.tt(gr[:, n, :], bank[:, :], s, ALU.mult, t, tg)
                                self.ps.give(b, t)
                            else:
                                t = self.tt(s, bank[:, :], s, ALU.mult, t, tg)
                                self.ps.give(b, t)
                                t = self.tt(s, s, gr[:, n, :], ALU.add)
                                t = self.split(self.ah[:, 4 * half + n, :], self.al[:, 4 * half + n, :], s, t)
                                merged.append(t)
                            self.scr_ring.done(i, t)
                        self.lin(A[name][0], 0, 4, c, lambda k, br=br: (yh[:, 4 * br + k, :], yl[:, 4 * br + k, :]),
                                 evac, ty)
                self.scale_x(alpha)

                def evac(n, b, bank, t):
                    self.xt[n] = self.stt(self.x[:, n, :], bank[:, :], self.mod(2, n), self.x[:, n, :], ALU.mult,
                                          ALU.add, t)
                    self.ps.give(b, self.xt[n])
                self.lin(A["w_out_3"][0], 0, 8, [128 * n for n in range(8)], self.xact, evac, merged)
                self.barrier()

    def stick(self, q, k, v, yS, sc):
        NB, G = 8, 4
        ab = [self.sb("ab", [128, 512], F, sc) for _ in range(G)]
        rs = [self.sb("rs", [128, 512], F, sc) for _ in range(NB)]
        place = self.borrow({f"{n}{i}": [512] for n in ("sp", "mb", "lw") for i in range(NB)})
        sp, mb, lw = ([place[f"{n}{i}"] for i in range(NB)] for n in ("sp", "mb", "lw"))
        units = [dict(h=h, j=j) for h in range(8) for j in (3, 2, 1, 0)]
        free_mb, free_rs, free_lw, free_sp = [None] * NB, [None] * NB, [None] * NB, [None] * NB
        held = {}

        def s_scores(i, u):
            h, j = u["h"], u["j"]
            hs = slice(64 * (h % 2), 64 * (h % 2) + 64)
            n = 512 - 128 * j
            b, bank, free = self.ps.take()
            t = self.mma(bank[:, 0:n], k[hs, h // 2, 128 * j:128 * j + 128], q[hs, h // 2, 128 * j:512], True, True,
                         free, inc=True)
            a = ab[i % G][:, 0:n]
            self.func(a, bank[:, 0:n], ACT.Abs, t)
            self.func(a, a, ACT.Exp, scale=-1.0)
            u["b"], u["bank"], u["n"] = b, bank, n

        def s_logs(i, u):
            n = u["n"]
            u["t"] = self.func(sp[i % NB][:, 0:n], ab[i % G][:, 0:n], ACT.Ln, free_sp[i % NB], bias=self.ones[:, 0:1])

        def s_sums(i, u):
            n, j, bank = u["n"], u["j"], u["bank"]
            s, m, l, r = (x[i % NB] for x in (sp, mb, lw, rs))
            self.stt(m[:, 0:n], bank[:, 0:n], 0.0, s[:, 0:n], ALU.max, ALU.add, u["t"], free_mb[i % NB])
            self.tt(m[:, 0:128], m[:, 0:128], self.c("before"), ALU.mult)
            t = self.stt(l[:, 0:n], bank[:, 0:n], 0.0, s[:, 0:n], ALU.min, ALU.subtract, free_lw[i % NB])
            self.ps.give(u["b"], t)
            free_sp[i % NB] = t
            u["r"] = rs[(i - 1) % NB] if j < 3 else None
            if j:
                t = self.V(lambda e: e.tensor_copy(r[:, 128 * j:128 * j + 128], m[:, 0:128]), free_rs[i % NB])
                if j < 3:
                    p = rs[(i - 1) % NB]
                    t = self.tt(r[:, 128 * (j + 1):512], m[:, 128:n], p[:, 128 * (j + 1):512], ALU.add)
            u["t"] = t

        def s_after(i, u):
            n, j = u["n"], u["j"]
            m, l = mb[i % NB], lw[i % NB]
            b, bank, free = self.ps.take()
            t = self.mma(bank[:, 0:n], self.c("after"), m[:, 0:n], True, j == 3, free, u["t"], inc=True)
            if j < 3:
                t = self.mma(bank[:, 128:n], self.ones, u["r"][:, 128 * (j + 1):512], False, True, inc=True)
                free_rs[(i - 1) % NB] = t
            free_mb[i % NB] = t
            t = self.tt(l[:, 0:n], l[:, 0:n], bank[:, 0:n], ALU.subtract, t)
            self.ps.give(b, t)
            u["t"] = self.func(l[:, 0:n], l[:, 0:n], ACT.Exp, t)

        def s_values(i, u):
            n, j, h = u["n"], u["j"], u["h"]
            l = lw[i % NB]
            t = self.tt(l[:, 0:128], l[:, 0:128], self.c("before"), ALU.mult, u["t"])
            if h // 2 not in held:
                held[h // 2] = self.bank()
            b, bank = held[h // 2]
            hs = slice(64 * (h % 2), 64 * (h % 2) + 64)
            t = self.mma(bank[hs, 128 * j:512], v[:, j, 64 * h:64 * h + 64], l[:, 0:n], j == 3, j == 0, t, inc=True)
            free_lw[i % NB] = t
            if h % 2 == 1 and j == 0:
                self.ps.give(b, self.func(yS[:, h // 2, :], bank[:, :], ACT.Copy, t))

        ng = len(units) // G
        for s in range(ng + 3):
            for lag, stage in ((3, s_values), (2, s_after), (1, s_sums), (0, s_scores), (0, s_logs)):
                if 0 <= s - lag < ng:
                    for i in range(G * (s - lag), G * (s - lag) + G):
                        stage(i, units[i])
        self.give_back(self.pe.tok(), self.act.tok(), self.dve.tok())

    def exact_exp(self, o, x, r, y, n, ni):
        self.ts(r, x, -87.3, 88.0, ALU.max, ALU.min)
        self.ts(n, r, 1.4426950408889634, None, ALU.mult, None)
        self.ts(n, n, 12582912.0, None, ALU.add, None)
        self.ts(n, n, 12582912.0, None, ALU.subtract, None)
        for c in (0.693145751953125, 1.428606765330187e-06):
            self.stt(r, n, -c, r, ALU.mult, ALU.add)
        f = [1.0]
        for i in range(1, 8):
            f.append(f[-1] / i)
        self.ts(y, r, f[7], f[6], ALU.mult, ALU.add)
        for i in range(5, -1, -1):
            self.tt(y, y, r, ALU.mult)
            self.ts(y, y, f[i], None, ALU.add, None)
        self.ts(n, n, 127.0, None, ALU.add, None)
        self.V(lambda e: e.tensor_copy(ni[:, :], n))
        self.V(lambda e: e.tensor_scalar(ni[:, :], ni[:, :], 23, None, ALU.logical_shift_left))
        return self.tt(o, y, ni[:, :].bitcast(F), ALU.mult)

    def cmul(self, o, a, b, tmp, n=None):
        self.tt(o[0], a[0], b[0], ALU.mult)
        self.tt(tmp, a[1], b[1], ALU.mult)
        self.tt(o[0], o[0], tmp, ALU.subtract)
        self.tt(o[1], a[0], b[1], ALU.mult)
        self.tt(tmp, a[1], b[0], ALU.mult)
        return self.tt(o[1], o[1], tmp, ALU.add)

    def ssm_tables(self, ctx):
        sb = lambda n, s, dt=F: self.sb(n, s, dt, ctx)
        self.ssm_t = dict(sp=sb("ssmp", [128, NSSM]), small=sb("small", [128, 18, 16]), ni=sb("ni", [128, 16], mybir.dt.int32),
                          L=[sb("Lr", [128, 9, 16]), sb("Li", [128, 9, 16])],
                          bb=[sb("bbr", [128, 16, 16]), sb("bbi", [128, 16, 16])],
                          T=[sb("Tc", [128, 16, 64]), sb("Ts", [128, 16, 64])], rho=sb("rho", [128, 16, 64]))

    def ssm_setup(self):
        sp, small, ni, L, bb, T, rho = (self.ssm_t[n] for n in ("sp", "small", "ni", "L", "bb", "T", "rho"))
        P = lambda n: sp[:, SSM[n][0]:SSM[n][0] + SSM[n][1]]
        self.dve.wait(self.actdma(sp[:, :], self.A["ssm"]))
        self.act.wait((self.s_in, self.n_in))
        self.ts(P("c_im"), P("c_im"), -1.0, None, ALU.mult, None)
        S = lambda i: small[:, i, :]
        dt, zr, zi, nn, co, si, mg, m8, fr, fi, x0, x1, er, ei, e2r, e2i, den, one = (S(i) for i in range(18))
        self.exact_exp(dt, P("log_dt"), x0, x1, nn, ni)
        self.tt(zr, P("a_re"), dt, ALU.mult)
        yield
        self.tt(zi, P("a_im"), dt, ALU.mult)
        self.exact_exp(mg, zr, x0, x1, nn, ni)
        yield
        self.tt(m8, mg, mg, ALU.mult)
        self.tt(m8, m8, m8, ALU.mult)
        yield
        self.tt(m8, m8, m8, ALU.mult)
        self.ts(nn, zi, 0.15915494309189535, None, ALU.mult, None)
        self.ts(nn, nn, 12582912.0, None, ALU.add, None)
        yield
        self.ts(nn, nn, 12582912.0, None, ALU.subtract, None)
        for c in (6.28125, 0.0019350051879882812, 3.019916050561733e-07):
            self.stt(zi, nn, -c, zi, ALU.mult, ALU.add)
        t = self.ts(zi, zi, 3.1415925, -3.1415925, ALU.min, ALU.max)
        yield
        self.func(si, zi, ACT.Sin, t)
        t = self.func(x0, zi, ACT.Abs)
        yield
        t = self.ts(x0, x0, -1.0, 1.5707963267948966, ALU.mult, ALU.add, t)
        t = self.func(co, x0, ACT.Sin, t)
        tmp = self.rb
        pw = lambda s: (L[0][:, s, :], L[1][:, s, :])
        self.V(lambda e: e.memset(L[0][:, 0, :], 1.0), t)
        self.V(lambda e: e.memset(L[1][:, 0, :], 0.0))
        yield
        self.tt(L[0][:, 1, :], mg, co, ALU.mult)
        self.tt(L[1][:, 1, :], mg, si, ALU.mult)
        yield
        t16 = tmp[:, 0:16]
        b4 = lambda ap, n: ap.to_broadcast([128, n, 16])
        yield
        self.cmul(pw(2), pw(1), pw(1), t16)
        for lo in (2, 4):
            w = [b4(L[i][:, lo:lo + 1, :], lo) for i in range(2)]
            self.cmul([L[i][:, lo + 1:2 * lo + 1, :] for i in range(2)], [L[i][:, 1:lo + 1, :] for i in range(2)],
                      w, tmp[:, 0:16 * lo].rearrange("p (a b) -> p a b", a=lo))
            yield
        ar, ai = P("a_re"), P("a_im")
        yield
        self.tt(den, ar, ar, ALU.mult)
        self.tt(x0, ai, ai, ALU.mult)
        yield
        self.tt(den, den, x0, ALU.add)
        self.recip(den, den)
        yield
        self.ts(one, L[0][:, 1, :], -1.0, None, ALU.add, None)
        li = L[1][:, 1, :]
        self.tt(fr, one, ar, ALU.mult)
        self.tt(x0, li, ai, ALU.mult)
        yield
        self.tt(fr, fr, x0, ALU.add)
        self.tt(fr, fr, den, ALU.mult)
        yield
        self.tt(fi, li, ar, ALU.mult)
        self.tt(x0, one, ai, ALU.mult)
        yield
        self.tt(fi, fi, x0, ALU.subtract)
        self.tt(fi, fi, den, ALU.mult)
        yield
        p3 = lambda n: P(n).rearrange("p (q c) -> p q c", q=16)
        self.cmul([x[:, :, :] for x in bb], [x.unsqueeze(2).to_broadcast([128, 16, 16]) for x in (fr, fi)],
                  [p3("b_re"), p3("b_im")], tmp[:, 0:256].rearrange("p (q c) -> p q c", q=16))
        yield
        self.cmul((er, ei), (co, si), (co, si), t16)
        yield
        self.cmul((e2r, e2i), (er, ei), (er, ei), t16)
        self.cmul((er, ei), (e2r, e2i), (e2r, e2i), t16)
        yield
        self.V(lambda e: e.memset(T[0][:, :, 0:1], 1.0))
        self.V(lambda e: e.memset(T[1][:, :, 0:1], 0.0))
        yield
        cur, nxt = (er, ei), (e2r, e2i)
        for l in range(6):
            n = 2 ** l
            self.cmul([x[:, :, n:2 * n] for x in T], [x[:, :, 0:n] for x in T],
                      [x.unsqueeze(2).to_broadcast([128, 16, n]) for x in cur],
                      tmp[:, 0:16 * n].rearrange("p (q m) -> p q m", q=16))
            yield
            if l < 5:
                self.cmul(nxt, cur, cur, t16)
                yield
                cur, nxt = nxt, cur
        m8b = m8.unsqueeze(2).to_broadcast([128, 16, 64])
        self.V(lambda e: e.tensor_copy(rho[:, :, :], m8b))
        self.V(lambda e: e.memset(rho[:, :, 0:1], 0.0))
        yield

    def ssm(self, u, yM):
        with ExitStack() as sc:
            sb = lambda n, s: self.sb(n, s, F, sc)
            sp, L, bb, T, rho = (self.ssm_t[n] for n in ("sp", "L", "bb", "T", "rho"))
            p3 = lambda n: sp[:, SSM[n][0]:SSM[n][0] + SSM[n][1]].rearrange("p (q c) -> p q c", q=16)
            shapes = dict(XB0=[4, 8, 32], XB1=[4, 8, 32], WC0=[4, 9, 32], WC1=[4, 9, 32], XT=[4, 2, 2, 128],
                          TM=[4, 2, 256], KS=[4, 256])
            tmps = dict(d0=[4, 8, 16], d1=[4, 8, 16], g0=[4, 9, 16], g1=[4, 9, 16])
            far = self.borrow({**shapes, **tmps})
            slots = [{n: sb(n, [128, *s]) for n, s in shapes.items()}, far]
            U4, Y1 = sb("U4", [128, 4, 512]), sb("Y1", [64, 8, 4, 32])
            for i in range(4):
                self.dve.wait(*self.scr_ring.toks[i])
            G, G2 = ([self.scr[i][:, 256 * n:256 * n + 256] for n in range(2)] for i in range(2))
            H = [sb("H", [128, 4, 65]) for _ in range(2)]
            toks = [x for i in range(self.NSPL) for x in self.spl_ring.toks[i]]
            for n in ("XB0", "XB1", "WC0", "WC1", "TM"):
                self.V(lambda e, x=slots[0][n]: e.memset(x[:, :, :, :], 0.0))
                tg = self.pool.op(lambda e, x=far[n]: e.memset(x[:, :, :, :], 0.0), *toks)
            for x in H:
                tz = self.V(lambda e, x=x: e.memset(x[:, :, 0:1], 0.0))
            s_u, s_t = self.sem("s_u"), [self.sem("s_t0"), self.sem("s_t1")]
            n_u, n_t = [0], [0, 0]
            ends = [(self.pe.tok(), tz)] * 2
            w = self.rb[:, 0:256]
            t_u4 = [()]

            def load_u(j):
                self.act.wait(*t_u4[0])
                for a in range(4):
                    for q in range(4):
                        self.act.dma(lambda e, a=a, q=q: e.dma_start(
                            U4[32 * a:32 * a + 32, q, a:512], u[32 * q:32 * q + 32, j, 0:512 - a]), s_u)
                        n_u[0] += 16

            def prep(j):
                js, S, sl = slice(4 * j, 4 * j + 4), slots[j % 2], j % 2
                XB, WC, XT, TM, KS = [S["XB0"], S["XB1"]], [S["WC0"], S["WC1"]], S["XT"], S["TM"], S["KS"]
                for q in (self.dve, self.pool, self.act):
                    q.wait(*ends[sl], tz, tg)

                def outer(tt, o, w, n, tmp, sub):
                    sh = [128, 4, n, 16]
                    l = [x[:, 0:n, js].rearrange("p s q -> p q s").unsqueeze(3).to_broadcast(sh) for x in L]
                    x = [x[:, js, :].unsqueeze(2).to_broadcast(sh) for x in w]
                    t0, t1 = (y[:, :, :, :] for y in tmp)
                    for i, (a, b) in enumerate(((0, 0), (0, 1))):
                        tt(t0, l[0], x[i], ALU.mult)
                        tt(t1, l[1], x[1 - i], ALU.mult)
                        op = ALU.subtract if (i == 0) == sub else ALU.add
                        for g in range(2):
                            hs = slice(64 * g, 64 * g + 64)
                            t = tt(o[i][hs, :, 0:n, 16 * g:16 * g + 16], t0[hs], t1[hs], op)
                        yield t
                ptt = lambda o, a, b, op: self.pool.op(lambda e: e.tensor_tensor(o, a, b, op))
                xs = outer(self.tt, XB, bb, 8, (far["d0"], far["d1"]), True)
                ws = outer(ptt, WC, [p3("c_re"), p3("c_im")], 9, (far["g0"], far["g1"]), False)
                for tx, tw in zip(xs, ws):
                    yield
                self.pe.wait(tx)
                for q in range(4):
                    b, bank = self.bank()
                    for i in range(4):
                        bl, ri = i // 2, i % 2
                        t = self.tr(bank[:, 128 * i:128 * i + 128],
                                    XB[ri][:, q, 4 * bl:4 * bl + 4, :].rearrange("p s c -> p (s c)"), self.ident,
                                    inc=True)
                    yield
                    self.ps.give(b, self.func(XT[:, q, :, :, :].rearrange("p a b n -> p (a b n)"), bank[:, :],
                                              ACT.Copy, t))
                self.pe.wait(tw)
                for q2 in range(2):
                    b, bank = self.bank()
                    for i in range(2):
                        q = 2 * q2 + i
                        for ri in range(2):
                            t = self.mma(bank[0:32, 256 * i:256 * i + 256], XB[ri][:, q, 0, :],
                                         WC[ri][:, q, 0:8, :].rearrange("p s c -> p (s c)"), ri == 0, ri == 1,
                                         inc=True)
                    yield
                    self.ps.give(b, self.func(KS[0:32, 2 * q2:2 * q2 + 2, :].rearrange("p q n -> p (q n)"),
                                              bank[0:32, :], ACT.Copy, t))
                S["t"] = tk = self.act.tok()
                for s in range(8):
                    a, bl = s % 4, s // 4
                    self.act.dma(lambda e, s=s, a=a, bl=bl: e.dma_start(
                        TM[32 * a:32 * a + 32, :, bl, 32 * (7 - s):256], KS[0:32, :, 0:32 * (s + 1)]), s_t[sl], tk)
                    n_t[sl] += 16

            def run(j):
                js, S, sl = slice(4 * j, 4 * j + 4), slots[j % 2], j % 2
                WC, XT, TM = [S["WC0"], S["WC1"]], S["XT"], S["TM"]
                self.pe.wait((s_u, n_u[0]), S["t"])
                vb = [self.bank() for _ in range(2)]
                for q in range(4):
                    for ri in range(2):
                        for bl in range(2):
                            t = self.mma(vb[ri][1][:, 64 * q:64 * q + 64], XT[:, q, bl, ri, :],
                                         U4[:, q, 7 - 4 * bl:512:8], bl == 0, bl == 1, inc=True)
                yield
                tc, ts = (x[:, js, :].rearrange("p q m -> p (q m)") for x in T)
                vr, vi = vb[0][1][:, 0:256], vb[1][1][:, 0:256]
                gr, gi, hr, hi = *G, *G2
                self.tt(gr, vr, tc, ALU.mult, t)
                self.tt(w, vi, ts, ALU.mult)
                self.tt(gr, gr, w, ALU.add)
                self.tt(gi, vi, tc, ALU.mult)
                t = self.tt(w, vr, ts, ALU.mult)
                for b, _ in vb:
                    self.ps.give(b, t)
                self.tt(gi, gi, w, ALU.subtract)
                rh = rho[:, js, :].rearrange("p q m -> p (q m)")
                self.V(lambda e: e.tensor_tensor_scan(hr, rh, gr, 0.0, ALU.mult, ALU.add))
                self.V(lambda e: e.tensor_tensor_scan(hi, rh, gi, 0.0, ALU.mult, ALU.add))
                q3 = lambda ap: ap.rearrange("p (q m) -> p q m", q=4)
                self.dve.wait(*t_u4[0])
                t = self.cmul([x[:, :, 1:65] for x in H], [q3(hr), q3(hi)], [x[:, js, :] for x in T], q3(w))
                self.pe.wait((s_t[sl], n_t[sl]))
                self.act.wait(*t_y1[0])
                for q2 in range(2):
                    b, bank = self.bank()
                    for i in range(2):
                        q = 2 * q2 + i
                        o = bank[0:64, 256 * i:256 * i + 256]
                        for bl in range(2):
                            self.mma(o, U4[:, q, 7 - 4 * bl:512:8], TM[:, q, bl, :], bl == 0, False)
                        for ri in range(2):
                            t2 = self.mma(o, H[ri][:, q, 0:64], WC[ri][:, q, 1:9, :].rearrange("p s c -> p (s c)"),
                                          False, ri == 1, t, inc=True)
                    if q2:
                        ends[sl] = t_u4[0] = (t2,)
                        if j < 3:
                            load_u(j + 1)
                    yield
                    ty = self.func(Y1[:, :, 2 * q2:2 * q2 + 2, :].rearrange("p i q c -> p q i c"),
                                   bank[0:64, :].rearrange("p (q i c) -> p q i c", q=2, i=8), ACT.Copy, t2)
                    self.ps.give(b, ty)
                b, bank = self.bank()
                for i in range(8):
                    t2 = self.tr(bank[:, 64 * i:64 * i + 64], Y1[:, i, :, :].rearrange("p q c -> p (q c)"),
                                 self.ident[0:64, 0:64], ty, inc=True)
                t_y1[0] = (t2,)
                yield
                y3 = yM[:, j, :].rearrange("p (m i) -> p m i", i=8)
                t = self.stt(y3, u[:, j, :].rearrange("p (m i) -> p m i", i=8), self.p("ssm_d", j),
                             bank[:, :].rearrange("p (i m) -> p m i", i=8), ALU.mult, ALU.add, t2)
                self.ps.give(b, t)
                self.func(yM[:, j, :], yM[:, j, :], ACT.Gelu_apprx_tanh, t)

            t_y1 = [()]
            load_u(0)
            for j in range(5):
                for _ in self.rounds(([run(j - 1)] if j else []) + ([prep(j)] if j < 4 else [])):
                    pass
            self.give_back(self.pe.tok(), self.act.tok(), self.dve.tok(), self.pool.tok())
            self.barrier()
            for i in range(4):
                self.scr_ring.done(i, self.dve.tok())
def _constants():
    i = np.arange(128)
    q, k = i[:, None], i[None, :]
    c = {}
    c["ident"] = np.eye(128)
    c["ones"] = np.ones((128, 128))
    c["bones"] = (q // 64 == k // 64)
    c["causal"] = np.where(k <= q, 0.0, -1e30)
    c["swaprev"] = np.where(k > q, 0.0, -1e30)
    c["after"] = (q > k)
    c["before"] = (q < k)
    t = 128 * np.arange(4)[None, :, None] + i[:, None, None]
    c["cmpmask"] = np.where(16 * np.arange(31)[None, None, :] + 31 <= t, 0.0, -1e30).reshape(128, 124)
    c["rowok"] = (i[:, None] >= 31)
    c["eps6"] = np.full((128, 1), 1e-6)
    c["eps5"] = np.full((128, 1), 1e-5)
    c["epsg"] = np.full((128, 1), 64e-5)
    s, u = i[:, None] % 64, i[None, :]
    c["gram"] = np.where(u < 64, (s < u) & (i[:, None] >= 64), s <= u - 64)
    c["upper"] = (s < u)[:, :64]
    for l in range(6):
        b = 2 ** l
        c[f"lev{l}"] = (q // (2 * b) == k // (2 * b)) & (q % (2 * b) < b) & (k % (2 * b) >= b)
        c[f"lev{l}"] = c[f"lev{l}"] & (q // 64 == k // 64)
    return {n: np.asarray(a, np.float32) for n, a in c.items()}


def _place(items):
    at, o = {}, 0
    for n, w in items:
        at[n] = (o, w)
        o += w
    return at, o


CONST = _constants()
_RW = [n for n in CONST if n in ("gram", "upper") or n.startswith("lev")]
CST, NCST = _place([(n, a.shape[1]) for n, a in CONST.items() if n not in _RW])
RWC, NRWC = _place([(n, CONST[n].shape[1]) for n in _RW])


def _cols(v):
    return np.asarray(v).reshape(-1, 128).T


def _params(I):
    dup = lambda v: np.concatenate([v, v])[:, None]
    z = lambda n: np.zeros(n, np.float32)
    P = {}
    P["norm_mix_g0"], P["norm_mix_g1"] = _cols(I["norm_mix_g"][0]), _cols(I["norm_mix_g"][1])
    P["norm_mlp_g0"], P["norm_mlp_g1"] = _cols(I["norm_mlp_g"][0]), _cols(I["norm_mlp_g"][1])
    P["mem_norm_g"] = _cols(I["mem_norm_g"])
    P["mem_q_norm_g0"], P["mem_q_norm_g1"] = dup(I["mem_q_norm_g"][0]), dup(I["mem_q_norm_g"][1])
    P["mem_k_norm_g"] = np.stack([np.tile(I["mem_k_norm_g"][l], 2) for l in range(2)], 1)
    P["a_b_glu"] = _cols(I["a_b_glu"][0])
    P["a_dw"] = I["a_dw"][0].reshape(31, 6, 128).transpose(2, 1, 0).reshape(128, 186)
    for n in ("a_dw_b", "a_ln_g", "a_ln_b"):
        P[n] = _cols(I[n][0])
    P["b_gate_b"] = np.concatenate([z(92), I["b_gate_b"][0]])[:, None]
    P["b_q_norm_g"] = dup(I["b_q_norm_g"][0])
    P["kv_norm_g"] = _cols(I["kv_norm_g"])
    for i in range(3):
        P[f"k_norm_g{i}"] = dup(I["k_norm_g"][i])
    P["pe_k"] = I["cmp_pe_k"].reshape(16, 128).T
    P["pe_v"] = I["cmp_pe_v"].reshape(16, 128).T
    for n in ("ffn1_norm", "mix_norm", "ffn2_norm", "final_norm", "rwkv_w0", "rwkv_a0", "rwkv_k_k", "rwkv_k_a",
              "rwkv_ln_w", "rwkv_ln_b"):
        P[n] = _cols(I[n + "_2"][0])
    P["rwkv_r_k"] = _cols(I["rwkv_r_k_2"][0].reshape(512))
    P["mu"] = _cols(np.concatenate([I["rwkv_mu_2"][0], z(96)]))
    P["attn_q_norm"], P["attn_k_norm"] = dup(I["attn_q_norm_2"][0]), dup(I["attn_k_norm_2"][0])
    P["sinks"] = np.repeat(I["attn_sinks_2"][0][None, :], 128, 0)
    P["c"] = _cols(I["c_3"][0])
    P["b_ada"] = _cols(I["b_ada_3"][0])
    for n in ("ssm_d", "b_glu", "ln1_g", "ln1_b", "ln2_g", "ln2_b"):
        P[n] = _cols(I[n + "_3"][0])
    return P


def _ssm(I):
    S = {}
    pair = lambda a: a.reshape(16, 2, 64, -1).transpose(1, 2, 0, 3).reshape(128, -1)
    S["a_re"], S["a_im"] = pair(I["ssm_a_re_3"][0]), pair(I["ssm_a_im_3"][0])
    S["log_dt"] = pair(np.repeat(I["ssm_log_dt_3"][0][:, None], 64, 1))
    S["b_re"], S["b_im"] = pair(I["ssm_b_re_3"][0]), pair(I["ssm_b_im_3"][0])
    S["c_re"] = pair(I["ssm_c_re_3"][0].transpose(0, 2, 1))
    S["c_im"] = pair(I["ssm_c_im_3"][0].transpose(0, 2, 1))
    return S


_PARW = dict(norm_mix_g0=8, norm_mix_g1=8, norm_mlp_g0=8, norm_mlp_g1=8, mem_norm_g=8, mem_q_norm_g0=1,
             mem_q_norm_g1=1, mem_k_norm_g=2, a_b_glu=12, a_dw=186, a_dw_b=6, a_ln_g=6, a_ln_b=6, b_gate_b=1,
             b_q_norm_g=1, kv_norm_g=8, k_norm_g0=1, k_norm_g1=1, k_norm_g2=1, pe_k=16, pe_v=16, ffn1_norm=8,
             mix_norm=8, ffn2_norm=8, final_norm=8, rwkv_w0=4, rwkv_a0=4, rwkv_k_k=4, rwkv_k_a=4, rwkv_ln_w=4,
             rwkv_ln_b=4, rwkv_r_k=4, mu=14, attn_q_norm=1, attn_k_norm=1, sinks=8, c=8, b_ada=48, ssm_d=4,
             b_glu=4, ln1_g=8, ln1_b=8, ln2_g=8, ln2_b=8)
PAR, NPAR = _place(list(_PARW.items()))
_SSMW = dict(a_re=16, a_im=16, log_dt=16, b_re=256, b_im=256, c_re=256, c_im=256)
SSM, NSSM = _place(list(_SSMW.items()))


def _pack(P, widths):
    for n, w in widths.items():
        assert P[n].shape == (128, w), (n, P[n].shape)
    return np.ascontiguousarray(np.concatenate([P[n] for n in widths], 1))
def program(nc, A, out, blocks):
    with ExitStack() as ctx:
        net = Net(nc, ctx)
        net.rb = net.sb("rb", [128, 512])
        net.setup(A)
        net.ready()
        if 1 not in blocks:
            for q in (net.pe, net.act, net.dve):
                q.wait(*net.xt)
        if 3 in blocks:
            net.modulation()
        if 1 in blocks:
            net.block1()
        if 2 in blocks:
            net.block2()
        if 3 in blocks:
            net.block3()
        s_out = net.sem("s_out")
        for k in range(8):
            net.sp.dma(lambda e, k=k: e.dma_start(out[128 * k:128 * k + 128, :], net.x[:, k, :]), s_out,
                       net.dve.tok(), net.act.tok())
        net.sp.wait((s_out, 128))
        block = ctx.enter_context(nc.Block())
        block.sync(lambda e: net.sp.emit(e))
        block.gpsimd(lambda e: net.pool.emit(e))
        block.scalar(lambda e: net.act.emit(e))
        block.vector(lambda e: net.dve.emit(e))
        block.tensor(lambda e: net.pe.emit(e))
        return net


WEIGHTS = [n for n in """w_mem_kv w_out w_mlp_in w_mlp_out a_w_in b_w_in w_kv cmp_w1_k cmp_w2_k cmp_w1_v cmp_w2_v
ffn1_w_gate_2 ffn1_w_up_2 ffn1_w_down_2 w_in_2 rwkv_w_lora_up_2 rwkv_a_lora_up_2 rwkv_g_lora_up_2 w_branch_rwkv_2
w_branch_attn_2 w_out_2 ffn2_w_gate_2 ffn2_w_up_2 ffn2_w_down_2 w_ada_3 w_in_3 w_sb_up_3 w_glu_3 w_ssm_up_3 w_out_3
w_ffn_in_3 w_ffn_out_3""".split()]


def arrays(I):
    a = {n: np.ascontiguousarray(I[n]) for n in WEIGHTS}
    a["xT"] = np.ascontiguousarray(np.asarray(I["x"])[0].T)
    a["memT"] = np.ascontiguousarray(np.asarray(I["mem"])[0].T)
    a["par"] = _pack(_params(I), _PARW)
    a["ssm"] = _pack(_ssm(I), _SSMW)
    a["cst"] = np.ascontiguousarray(np.concatenate([CONST[n] for n in CST], 1))
    a["rwc"] = np.ascontiguousarray(np.concatenate([CONST[n] for n in RWC], 1))
    return a


def kernel(**inputs):
    import concourse.bacc as _bacc
    from concourse.bass_utils import run_bass_kernel_spmd as _run

    I = {n: np.asarray(v) for n, v in inputs.items()}
    a = arrays(I)
    nc = _bacc.Bacc("TRN2", target_bir_lowering=False, num_devices=1)
    A = {n: nc.dram_tensor(f"in_{n}", v.shape, mybir.dt.from_np(v.dtype), kind="ExternalInput").ap()
         for n, v in a.items()}
    out = nc.dram_tensor("out_0", (1024, 512), F, kind="ExternalOutput").ap()
    program(nc, A, out, (1, 2, 3))
    r = _run(nc, [{f"in_{n}": v for n, v in a.items()}], core_ids=[0])
    return np.ascontiguousarray(r.results[0]["out_0"].T)[None]
```
